# Optimizing a Trainium2 kernel written in Bass

```python
import jax, jax.numpy as jnp
from jax import lax
import numpy as np

D_MODEL = 1024
BATCH = 1
SEQ = 1024
DEPTH = 1

D_MIX = 1024
HEAD_DIM = 64
BLOCK = 128
A_HEADS = 8
A_KV_HEADS = 2
A_REP = A_HEADS // A_KV_HEADS
A_WIDTH = A_HEADS * HEAD_DIM
WINDOW = 128
B_HEADS = 8
B_NOPE = 64
B_ROPE = 32
B_V = 64
B_WIDTH = B_HEADS * B_V
Q_LORA = 384
KV_LORA = 256
ROPE_BASE = 10000.0
EPS = 1e-6

IN_SIZES = (
    A_WIDTH,
    A_KV_HEADS * HEAD_DIM,
    A_KV_HEADS * HEAD_DIM,
    A_WIDTH,
    Q_LORA,
    KV_LORA,
    B_ROPE,
    B_WIDTH,
)
IN_COLS = int(sum(IN_SIZES))

kernel_name = "hymba_swa_sink_alibi_mla_encoder"

def rmsnorm(x, gain):
    x32 = x.astype(jnp.float32)
    y = x32 * lax.rsqrt(jnp.mean(x32 * x32, axis=-1, keepdims=True) + EPS)
    return (y * gain.astype(jnp.float32)).astype(x.dtype)

def alibi_slopes(n_heads):
    return jnp.exp2(-8.0 * jnp.arange(1, n_heads + 1, dtype=jnp.float32) / n_heads)

def apply_rope(x, cos, sin):
    x1, x2 = jnp.split(x, 2, axis=-1)
    c = cos[None, :, None, :].astype(x.dtype)
    s = sin[None, :, None, :].astype(x.dtype)
    return jnp.concatenate([x1 * c - x2 * s, x1 * s + x2 * c], axis=-1)

def window_attention(q, k, v, sink):
    B, S = q.shape[0], q.shape[1]
    nb = S // BLOCK
    qb = q.reshape(B, nb, BLOCK, A_KV_HEADS, A_REP, HEAD_DIM)
    pad = ((0, 0), (BLOCK, BLOCK), (0, 0), (0, 0))
    kp = jnp.pad(k, pad).reshape(B, nb + 2, BLOCK, A_KV_HEADS, HEAD_DIM)
    vp = jnp.pad(v, pad).reshape(B, nb + 2, BLOCK, A_KV_HEADS, HEAD_DIM)
    kb = jnp.concatenate([kp[:, :-2], kp[:, 1:-1], kp[:, 2:]], axis=2)
    vb = jnp.concatenate([vp[:, :-2], vp[:, 1:-1], vp[:, 2:]], axis=2)

    scores = jnp.einsum('bnqgrd,bnkgd->bngrqk', qb, kb).astype(jnp.float32)
    scores = scores * (HEAD_DIM ** -0.5)

    qi = jnp.arange(BLOCK)[:, None]
    kj = jnp.arange(3 * BLOCK)[None, :]
    dist = jnp.abs(qi - kj + BLOCK).astype(jnp.float32)
    s_pos = (jnp.arange(nb)[:, None] * BLOCK - BLOCK + jnp.arange(3 * BLOCK)[None, :])
    valid_s = (s_pos >= 0) & (s_pos < S)
    mask = (dist <= WINDOW)[None] & valid_s[:, None, :]
    slopes = alibi_slopes(A_HEADS).reshape(A_KV_HEADS, A_REP)
    bias = -slopes[:, :, None, None] * dist[None, None]
    scores = jnp.where(mask[None, :, None, None], scores + bias[None, None], -jnp.inf)

    sink_l = sink.astype(jnp.float32).reshape(A_KV_HEADS, A_REP)[None, None, :, :, None, None]
    m = jnp.maximum(jnp.max(scores, axis=-1, keepdims=True), sink_l)
    p = jnp.exp(scores - m)
    denom = jnp.sum(p, axis=-1, keepdims=True) + jnp.exp(sink_l - m)
    probs = (p / denom).astype(v.dtype)
    out = jnp.einsum('bngrqk,bnkgd->bnqgrd', probs, vb)
    return out.reshape(B, S, A_WIDTH)

def latent_attention(q_nope, q_rope, k_nope, k_rope, v):
    B, S = q_nope.shape[0], q_nope.shape[1]
    nb = S // BLOCK
    scale = (B_NOPE + B_ROPE) ** -0.5
    qn = q_nope.reshape(B, nb, BLOCK, B_HEADS, B_NOPE).transpose(1, 0, 2, 3, 4)
    qr = q_rope.reshape(B, nb, BLOCK, B_HEADS, B_ROPE).transpose(1, 0, 2, 3, 4)

    def one_block(args):
        qn_b, qr_b = args
        s = (jnp.einsum('bqhd,bkhd->bhqk', qn_b, k_nope)
             + jnp.einsum('bqhr,bkr->bhqk', qr_b, k_rope)).astype(jnp.float32) * scale
        p = jax.nn.softmax(s, axis=-1).astype(v.dtype)
        return jnp.einsum('bhqk,bkhd->bqhd', p, v)

    out = lax.map(one_block, (qn, qr))
    return out.transpose(1, 0, 2, 3, 4).reshape(B, S, B_WIDTH)

def setup_inputs(seed: int = 0) -> dict:
    key = jax.random.key(seed)
    ks = jax.random.split(key, 12)
    f32 = jnp.float32
    x = jax.random.normal(ks[0], (BATCH, SEQ, D_MODEL), f32)
    norm_mix = 1.0 + 0.01 * jax.random.normal(ks[1], (DEPTH, D_MODEL), f32)
    w_in = jax.random.normal(ks[2], (DEPTH, D_MODEL, IN_COLS), f32) * D_MODEL ** -0.5
    attn_sink = 0.5 * jax.random.normal(ks[3], (DEPTH, A_HEADS), f32)
    q_a_norm = 1.0 + 0.01 * jax.random.normal(ks[4], (DEPTH, Q_LORA), f32)
    w_uq = jax.random.normal(ks[5], (DEPTH, Q_LORA, B_HEADS * (B_NOPE + B_ROPE)), f32) * Q_LORA ** -0.5
    kv_a_norm = 1.0 + 0.01 * jax.random.normal(ks[6], (DEPTH, KV_LORA), f32)
    w_ukv = jax.random.normal(ks[7], (DEPTH, KV_LORA, B_HEADS * (B_NOPE + B_V)), f32) * KV_LORA ** -0.5
    w_out = jax.random.normal(ks[8], (DEPTH, D_MIX, D_MODEL), f32) * D_MIX ** -0.5
    final_norm = 1.0 + 0.01 * jax.random.normal(ks[9], (D_MODEL,), f32)
    return {"x": x, "norm_mix": norm_mix, "w_in": w_in, "attn_sink": attn_sink,
            "q_a_norm": q_a_norm, "w_uq": w_uq, "kv_a_norm": kv_a_norm, "w_ukv": w_ukv,
            "w_out": w_out, "final_norm": final_norm}

def reference(x, norm_mix, w_in, attn_sink, q_a_norm, w_uq, kv_a_norm, w_ukv, w_out, final_norm):
    B, S = x.shape[0], x.shape[1]
    split_idx = np.cumsum(np.array(IN_SIZES))[:-1].tolist()
    pos = jnp.arange(S, dtype=jnp.float32)
    inv_freq = ROPE_BASE ** (-jnp.arange(0, B_ROPE, 2, dtype=jnp.float32) / B_ROPE)
    ang = pos[:, None] * inv_freq[None, :]
    cos, sin = jnp.cos(ang), jnp.sin(ang)

    for l in range(DEPTH):
        h = rmsnorm(x, norm_mix[l])
        proj = jnp.einsum('bsd,dc->bsc', h, w_in[l])
        qa, ka, va, ga, cq, ckv, kr, gb = jnp.split(proj, split_idx, axis=-1)

        ya = window_attention(qa.reshape(B, S, A_HEADS, HEAD_DIM),
                              ka.reshape(B, S, A_KV_HEADS, HEAD_DIM),
                              va.reshape(B, S, A_KV_HEADS, HEAD_DIM),
                              attn_sink[l])
        ya = ya * jax.nn.silu(ga)

        q = jnp.einsum('bsc,ce->bse', rmsnorm(cq, q_a_norm[l]), w_uq[l])
        q = q.reshape(B, S, B_HEADS, B_NOPE + B_ROPE)
        q_nope, q_rope = q[..., :B_NOPE], apply_rope(q[..., B_NOPE:], cos, sin)
        kv = jnp.einsum('bsc,ce->bse', rmsnorm(ckv, kv_a_norm[l]), w_ukv[l])
        kv = kv.reshape(B, S, B_HEADS, B_NOPE + B_V)
        k_nope, v_b = kv[..., :B_NOPE], kv[..., B_NOPE:]
        k_rope = apply_rope(kr.reshape(B, S, 1, B_ROPE), cos, sin)[:, :, 0, :]
        yb = latent_attention(q_nope, q_rope, k_nope, k_rope, v_b)
        yb = yb * jax.nn.silu(gb)

        y = jnp.concatenate([ya, yb], axis=-1)
        x = x + jnp.einsum('bsc,cd->bsd', y, w_out[l])

    return rmsnorm(x, final_norm)


_drawn_inputs = setup_inputs


def setup_inputs(seed=0):
    import zlib

    import numpy as np

    out = dict(_drawn_inputs(seed))
    spreads = {}
    factors = {'norm_mix': 8.0, 'attn_sink': 8.0, 'q_a_norm': 8.0, 'kv_a_norm': 8.0, 'final_norm': 5.694}
    for name, (base, spread) in spreads.items():
        noise = np.random.default_rng([zlib.crc32(name.encode()), seed]).standard_normal(out[name].shape)
        drawn = base * np.exp(spread * noise) if base else spread * noise
        out[name] = __import__('jax').numpy.asarray(drawn.astype(out[name].dtype))
    for name, factor in factors.items():
        out[name] = (out[name] * factor).astype(out[name].dtype)
    return out
```

```python
from contextlib import ExitStack

import numpy as np

import concourse.bass as bass
from concourse import mybir

F32 = mybir.dt.float32
F32R = mybir.dt.float32r
ALU = mybir.AluOpType
ACT = mybir.ActivationFunctionType
AX = mybir.AxisListType

P = 128
SEQ = 1024
D = 1024
NT = SEQ // P
KT = D // P
HALF = 512
HEADS = 8
HD = 64
GROUPS = 2
REP = HEADS // GROUPS
ROPE = 32
HR = ROPE // 2
QK = HD + ROPE
QL = 384
KVL = 256
QLT = QL // P
KVLT = KVL // P
LT = QLT + KVLT
A_SCALE = HD ** -0.5
B_SCALE = QK ** -0.5
EPS = 1e-6
MASKED = -1e30

QA, KA, VA, GA, CQ = 0, 512, 640, 768, 1280
CKV = CQ + QL
KR = CKV + KVL
GB = KR + ROPE
NA = P + KVL + ROPE
NW = NA + QL

BASE = 16512
SLOPE = [2.0 ** -(h + 1) for h in range(HEADS)]


def f(ap):
    return ap.bitcast(F32)


def encoder(nc, x, norm_mix, w_in, attn_sink, q_a_norm, w_uq, kv_a_norm, w_ukv, w_out, final_norm,
            rope_nat, rope_q, dist, out):
    q_scr = nc.dram_tensor("q_nope_scratch", [HEADS * HD, SEQ], F32, kind="Internal").ap()
    qr_scr = nc.dram_tensor("q_rope_scratch", [2, P, SEQ], F32, kind="Internal").ap()
    k_scr = nc.dram_tensor("k_nope_scratch", [HEADS * HD, SEQ], F32, kind="Internal").ap()
    kr_scr = nc.dram_tensor("k_rope_scratch", [ROPE, SEQ], F32, kind="Internal").ap()
    v_scr = nc.dram_tensor("v_scratch", [SEQ, HEADS * HD], F32, kind="Internal").ap()

    with ExitStack() as ctx:
        def sem(name):
            return ctx.enter_context(nc.semaphore(name))

        def at(name, kb, shape, dt=F32):
            return nc.alloc_sbuf_tensor_at(name, shape, dt, offset=BASE + int(kb * 1024))

        ident = at("ident", 0, [P, P])
        stat = at("stat", 0.5, [P, 96])
        sinkb = at("sinkb", 0.875, [P, HEADS])
        hT_hi = at("hT_hi", 1, [P, KT, SEQ], F32R)
        hT_lo = at("hT_lo", 33, [P, KT, SEQ], F32R)
        wn_hi = at("wn_hi", 65, [P, KT, NW], F32R)
        wn_lo = at("wn_lo", 90, [P, KT, NW], F32R)
        wn_raw = at("wn_raw", 115, [P, 3, NW])
        x_in = at("x_in", 124.5, [P, 2, D])
        x_n = at("x_n", 132.5, [P, 2, D])
        g_mix = at("g_mix", 140.5, [P, D])
        g_lat = at("g_lat", 144.5, [P, QL + KVL])
        lat = at("lat", 147, [P, 2, QL + KVL])
        kr_n = at("kr_n", 152, [P, NT, ROPE])
        kr_r = at("kr_r", 153, [P, NT, ROPE])
        kr_t = at("kr_t", 154, [P, 4, NT, HR])
        r_nat = at("r_nat", 156, [P, 2, NT, HR])
        vA = at("vA", 157, [P, NT, GROUPS, P], F32R)
        latT_hi = at("latT_hi", 165, [P, LT, SEQ], F32R)
        latT_lo = at("latT_lo", 185, [P, LT, SEQ], F32R)
        uq_raw = at("uq_raw", 115, [P, QLT, HEADS, QK])
        uq_hi = at("uq_hi", 124.5, [P, QLT, 6, P], F32R)
        uq_lo = at("uq_lo", 133.5, [P, QLT, 6, P], F32R)
        ukv_raw = at("ukv_raw", 65, [P, KVLT, HEADS, P])
        uk_hi = at("uk_hi", 73, [P, KVLT, HEADS, HD], F32R)
        uk_lo = at("uk_lo", 77, [P, KVLT, HEADS, HD], F32R)
        uv_hi = at("uv_hi", 81, [P, KVLT, HEADS, HD], F32R)
        uv_lo = at("uv_lo", 85, [P, KVLT, HEADS, HD], F32R)
        stage = at("stage", 89, [P, 4, HALF])
        r_tmp = at("r_tmp", 97, [P, 4, HALF])
        r_q = at("r_q", 105, [P, 2, SEQ])
        q_st = at("q_st", 65, [P, HEADS, SEQ], F32R)
        k_hi2 = at("k_hi2", 97, [P, GROUPS, SEQ], F32R)
        k_lo2 = at("k_lo2", 105, [P, GROUPS, SEQ], F32R)
        o_w = at("o_w", 113, [P, 2, 2, P])
        w_raw = at("w_raw", 115, [P, 2, KT, P])
        w_hi = at("w_hi", 124.5, [P, 2, KT, P], F32R)
        w_lo = at("w_lo", 132.5, [P, 2, KT, P], F32R)
        distb = at("distb", 140.5, [P, 3 * P])
        p_w = at("p_w", 142, [P, 2, REP, 3 * P])
        ol_w = at("ol_w", 154, [HD, HALF])
        pT_wh = at("pT_wh", 197, [P, 2, HALF], F32R)
        pT_wl = at("pT_wl", 201, [P, 2, HALF], F32R)
        Y = at("Y", 165, [P, KT, SEQ])
        v_raw = at("v_raw", 1, [P, NT, HEADS * HD])
        q_raw = at("q_raw", 17, [QK, SEQ])
        k_raw = at("k_raw", 21, [QK, SEQ])
        q_hi = at("q_hi", 25, [QK, 2, SEQ], F32R)
        q_lo = at("q_lo", 33, [QK, 2, SEQ], F32R)
        k_hi = at("k_hi", 41, [QK, 2, SEQ], F32R)
        k_lo = at("k_lo", 49, [QK, 2, SEQ], F32R)
        vB = at("vB", 57, [P, 2, NT, P], F32R)
        pT_hi = at("pT_hi", 65, [P, 2, NT, HALF], F32R)
        pT_lo = at("pT_lo", 97, [P, 2, NT, HALF], F32R)
        p_b = at("p_b", 129, [P, 3, SEQ])
        ol_b = at("ol_b", 141, [HD, HALF])
        o_b = at("o_b", 197, [P, 2, HALF])
        wo_raw = at("wo_raw", 145, [P, 4, D])
        y_hi = at("y_hi", 1, [P, KT, SEQ], F32R)
        y_lo = at("y_lo", 33, [P, KT, SEQ], F32R)
        wo_hi = at("wo_hi", 65, [P, KT, D], F32R)
        wo_lo = at("wo_lo", 97, [P, KT, D], F32R)
        x_r = at("x_r", 129, [P, 2, D])
        o_n = at("o_n", 137, [P, 2, D])
        g_fin = at("g_fin", 161, [P, D])

        ssq, var, rms, rstd = (stat[:, 8 * i:8 * i + 8] for i in range(4))
        lss, lvar, lrms, lrstd = (stat[:, 32 + 2 * i:34 + 2 * i] for i in range(4))

        def w_col(kind, u):
            c = 48 + 24 * (u % 2) + 4 * kind
            return stat[:, c:c + 4]

        nm_b, sum_b, r_b = (stat[:, 40 + 8 * 0 + 0:44], stat[:, 44:48], stat[:, 32:36])

        ps = ctx.enter_context(nc.psum_tensor("ps", [P, 8, HALF], F32))

        s_id = sem("ident_ready")
        s_gmix, s_glat, s_rnat, s_rq, s_sink, s_dist, s_gfin = (
            sem(n) for n in ("g_mix_in", "g_lat_in", "rope_nat_in", "rope_q_in", "sink_in", "dist_in",
                             "g_fin_in"))
        s_x = [sem(f"x_in{i}") for i in range(2)]
        s_wn = [sem(f"wn_in{i}") for i in range(3)]
        s_chain = sem("dve_chain")
        s_ssq, s_var, s_rms, s_xn = sem("ssq_ready"), sem("var_ready"), sem("rms_ready"), sem("xn_ready")
        s_xT, s_hhi, s_hT = sem("xT_done"), sem("hT_hi_ready"), sem("hT_ready")
        s_wnh, s_wnr = sem("wn_hi_ready"), sem("wn_ready")
        s_pA, s_pB = sem("natA_done"), sem("natB_done")
        s_va, s_lss, s_lvar, s_lrms, s_lat = (sem(n) for n in (
            "va_hi_ready", "lat_ssq_ready", "lat_var_ready", "lat_rms_ready", "lat_ready"))
        s_lT, s_lhi, s_latT = sem("lat_transposed"), sem("latT_hi_ready"), sem("latT_ready")
        s_krr = sem("k_rope_ready")
        s_uqi, s_ukvi = sem("uq_in"), sem("ukv_in")
        s_uqh, s_uq, s_ukvh, s_ukv = sem("uq_hi_ready"), sem("uq_ready"), sem("ukv_hi_ready"), sem("ukv_ready")
        s_up, s_upa, s_upd = sem("up_done"), sem("up_copied_act"), sem("up_copied_dve")
        s_st = [sem(f"stage_stored{i}") for i in range(4)]
        s_w = [sem(f"w_in{i}") for i in range(2)]
        s_wh, s_wr = sem("w_hi_ready"), sem("w_ready")
        s_g, s_ga, s_ge = sem("gated_done"), sem("gated_act"), sem("gated_evacuated")
        s_ws, s_wm, s_wnm, s_we, s_wrd, s_wp = (sem(n) for n in (
            "w_scores", "w_max", "w_negmax", "w_exp", "w_recip", "w_probs"))
        s_wT, s_wTh, s_wTl, s_wpv, s_wol, s_wo, s_wy = (sem(n) for n in (
            "w_transposed", "w_pT_hi", "w_pT_lo", "w_pv", "w_o_lo", "w_o", "w_y"))
        s_vr, s_krl, s_qki = sem("v_raw_in"), sem("k_rope_in"), sem("qk_raw_in")
        s_sph, s_sph2, s_sp, s_sp2 = sem("qk_hi_split"), sem("v_hi_split"), sem("qk_split"), sem("v_split")
        s_bs, s_bm, s_be, s_br, s_bp = (sem(n) for n in (
            "b_scores", "b_negmax", "b_exp", "b_recip", "b_probs"))
        s_bT, s_bTh, s_bTl, s_bpv, s_bol, s_bo, s_by = (sem(n) for n in (
            "b_transposed", "b_pT_hi", "b_pT_lo", "b_pv", "b_o_lo", "b_o", "b_y"))
        s_woi = [sem(f"wo_in{i}") for i in range(4)]
        s_yh, s_yl, s_woh, s_wol2 = sem("y_hi_ready"), sem("y_ready"), sem("wo_hi_ready"), sem("wo_ready")
        s_xr = [sem(f"x_again{i}") for i in range(2)]
        s_op, s_oadd, s_oss, s_ovar, s_orms, s_on = (sem(n) for n in (
            "out_projected", "out_added", "out_ssq", "out_var", "out_rms", "out_normed"))
        s_out = [sem(f"out_stored{i}") for i in range(2)]

        UP = [("r", 0, 0), ("r", 1, 0), ("r", 0, 1), ("r", 1, 1)]
        UP += [("q", j, h) for j in range(4) for h in range(2)]
        UP += [("kr", 0, 0), ("kr", 0, 1)]
        UP += [("k", j, h) for j in range(4) for h in range(2)]
        UP += [("v", st, 0) for st in range(NT)]
        BY_DVE = ("r", "v")
        N_Q = 12

        def wait_up_copied(eng, j):
            dve = UP[j][0] in BY_DVE
            n = sum(1 for k in UP[:j + 1] if (k[0] in BY_DVE) == dve)
            if UP[j][0] == "r" and UP[j][1] == 0:
                n += 1
            eng.wait_ge(s_upd if dve else s_upa, n)

        def wait_all_stored(eng):
            for i in range(4):
                eng.wait_ge(s_st[i], 16 * len(range(i, len(UP), 4)))

        M_COLS = [KA] + [QA + P * i for i in range(4)] + [GA + P * i for i in range(4)] \
            + [GB + P * i for i in range(4)]
        NM = len(M_COLS)
        N_WIN_JOB = 2 * (NM - 4)

        def g_bank(g):
            return 6 + g % 2 if g < N_WIN_JOB else 6

        def w_keys(u):
            n = u // GROUPS
            return range(max(n - 1, 0), min(n + 2, NT))

        W_UNITS = NT * GROUPS
        W_FIRST = [sum(len(w_keys(v)) for v in range(u)) for u in range(W_UNITS + 1)]

        B_UNITS = HEADS * NT
        B_GROUPS = B_UNITS // 4

        block = ctx.enter_context(nc.Block())

        @block.sync
        def _(sp):
            def load_x(t):
                if t >= 2:
                    sp.wait_ge(s_xn, t - 1)
                sp.dma_start(x_in[:, t % 2, :], x[t * P:(t + 1) * P, :]).then_inc(s_x[t % 2], 16)

            def load_wn(k):
                if k >= 3:
                    sp.wait_ge(s_wnr, k - 2)
                rows = w_in[k * P:(k + 1) * P, :]
                sp.dma_start(wn_raw[:, k % 3, 0:P], rows[:, VA:VA + P]).then_inc(s_wn[k % 3], 16)
                sp.dma_start(wn_raw[:, k % 3, P:NA], rows[:, CKV:CKV + KVL + ROPE]).then_inc(s_wn[k % 3], 16)
                sp.dma_start(wn_raw[:, k % 3, NA:NW], rows[:, CQ:CQ + QL]).then_inc(s_wn[k % 3], 16)

            load_x(0)
            sp.dma_start(g_mix[:, :], norm_mix.partition_broadcast(P)).then_inc(s_gmix, 16)
            load_x(1)
            load_wn(0)
            load_wn(1)
            load_wn(2)
            for t in range(2, NT):
                load_x(t)
                load_wn(t + 1) if t + 1 < KT else None
                if t == 3:
                    sp.dma_start(g_lat[:, 0:QL], q_a_norm.partition_broadcast(P)).then_inc(s_glat, 16)
                    sp.dma_start(g_lat[:, QL:QL + KVL], kv_a_norm.partition_broadcast(P)).then_inc(s_glat, 16)
                    sp.dma_start(r_nat[:, :, :, :], rope_nat).then_inc(s_rnat, 16)
                    sp.dma_start(sinkb[:, :], attn_sink.partition_broadcast(P)).then_inc(s_sink, 16)
            sp.wait_ge(s_wnr, KT)
            sp.dma_start(uq_raw[:, :, :, :],
                         w_uq.rearrange("(k p) (h c) -> p k h c", p=P, c=QK)).then_inc(s_uqi, 16)
            sp.wait_ge(s_pB, NT)
            sp.dma_start(ukv_raw[:, :, :, :],
                         w_ukv.rearrange("(k p) (h c) -> p k h c", p=P, c=P)).then_inc(s_ukvi, 16)
            sp.dma_start(r_q[:, :, :], rope_q).then_inc(s_rq, 16)

            def load_w(m):
                if m >= 2:
                    sp.wait_ge(s_wr, m - 1)
                elif m == 0:
                    sp.wait_ge(s_uq, 1)
                sp.dma_start(w_raw[:, m % 2, :, :],
                             w_in[:, M_COLS[m]:M_COLS[m] + P].rearrange("(k p) c -> p k c", p=P)) \
                    .then_inc(s_w[m % 2], 16)

            load_w(0)
            load_w(1)
            for j, (kind, t, h) in enumerate(UP):
                wait_up_copied(sp, j)
                src, cols = stage[:, j % 4, :], slice(h * HALF, (h + 1) * HALF)
                if kind == "r":
                    dst = qr_scr[t, :, cols]
                elif kind == "q":
                    dst = q_scr[t * P:(t + 1) * P, cols]
                elif kind == "kr":
                    dst, src = kr_scr[:, cols], stage[0:ROPE, j % 4, :]
                elif kind == "k":
                    dst = k_scr[t * P:(t + 1) * P, cols]
                else:
                    dst = v_scr[t * P:(t + 1) * P, :]
                sp.dma_start(dst, src).then_inc(s_st[j % 4], 16)
            sp.wait_ge(s_hT, NT)
            sp.dma_start(distb[:, :], dist).then_inc(s_dist, 16)
            for m in range(2, NM):
                load_w(m)

            wait_all_stored(sp)
            sp.wait_ge(s_g, 2 * NM)
            sp.dma_start(k_raw[HD:QK, :], kr_scr).then_inc(s_krl, 16)

            def load_qk(h):
                if h >= 1:
                    sp.wait_ge(s_sp, h)
                sp.dma_start(q_raw[0:HD, :], q_scr[h * HD:(h + 1) * HD, :]).then_inc(s_qki, 16)
                for i in range(2):
                    sp.dma_start(q_raw[HD + i * HR:HD + (i + 1) * HR, :],
                                 qr_scr[i, h * HR:(h + 1) * HR, :]).then_inc(s_qki, 16)
                sp.dma_start(k_raw[0:HD, :], k_scr[h * HD:(h + 1) * HD, :]).then_inc(s_qki, 16)

            load_qk(0)
            sp.dma_start(v_raw[:, :, :], v_scr.rearrange("(t p) c -> p t c", p=P)).then_inc(s_vr, 16)
            for h in range(1, HEADS):
                load_qk(h)

            def load_wo(k):
                if k >= 4:
                    sp.wait_ge(s_wol2, k - 3)
                sp.dma_start(wo_raw[:, k % 4, :], w_out[k * P:(k + 1) * P, :]).then_inc(s_woi[k % 4], 16)

            sp.wait_ge(s_wp, REP * W_UNITS)
            sp.wait_ge(s_wT, W_FIRST[W_UNITS])
            sp.wait_ge(s_wo, W_UNITS)
            for k in range(4):
                load_wo(k)
            sp.dma_start(g_fin[:, :], final_norm.partition_broadcast(P)).then_inc(s_gfin, 16)

            def load_again(t):
                if t == 0:
                    sp.wait_ge(s_bT, 2 * B_UNITS)
                if t >= 2:
                    sp.wait_ge(s_oss, t - 1)
                sp.dma_start(x_r[:, t % 2, :], x[t * P:(t + 1) * P, :]).then_inc(s_xr[t % 2], 16)

            load_again(0)
            load_again(1)
            for k in range(4, KT):
                load_wo(k)
            for t in range(NT):
                sp.wait_ge(s_on, t + 1)
                sp.dma_start(out[t * P:(t + 1) * P, :], o_n[:, t % 2, :]).then_inc(s_out[t % 2], 16)
                if t + 2 < NT:
                    load_again(t + 2)
            for i in range(2):
                sp.wait_ge(s_out[i], 16 * NT // 2)

        @block.gpsimd
        def _(pool):
            def split(raw, hi, lo, done_hi, n_hi, done):
                nc.gpsimd.tensor_scalar(hi, raw, 1.0, 1.0, ALU.mult, ALU.mult).then_inc(done_hi, 1)
                pool.wait_ge(done_hi, n_hi)
                last = nc.gpsimd.tensor_tensor(lo, raw, f(hi), ALU.subtract)
                if done is not None:
                    last.then_inc(done, 1)
                return last

            nc.gpsimd.memset(ident[:, :], 0.0).then_inc(s_id, 1)
            pool.wait_ge(s_id, 1)
            nc.gpsimd.affine_select(out=ident[:, :], in_=ident[:, :], compare_op=ALU.not_equal, fill=1.0,
                                    base=0, pattern=[[-1, P]], channel_multiplier=1).then_inc(s_id, 1)
            for k in range(KT):
                pool.wait_ge(s_wn[k % 3], 48 * (k // 3 + 1))
                split(wn_raw[:, k % 3, :], wn_hi[:, k, :], wn_lo[:, k, :], s_wnh, k + 1, s_wnr)
            pool.wait_ge(s_uqi, 16)
            pool.wait_ge(s_xT, NT)
            pool.wait_ge(s_hT, NT)
            for part in range(2):
                for k in range(QLT):
                    for dst, c, w in ((slice(0, 4), 0, HD), (4, HD, HR), (5, HD + HR, HR)):
                        hi, lo = uq_hi[:, k, dst, :], uq_lo[:, k, dst, :]
                        if w == HD:
                            hi, lo = (a.rearrange("p a (b c) -> p (a b) c", c=w) for a in (hi, lo))
                        else:
                            hi, lo = (a.rearrange("p (b c) -> p b c", c=w) for a in (hi, lo))
                        raw = uq_raw[:, k, :, c:c + w]
                        if part == 0:
                            last = nc.gpsimd.tensor_scalar(hi, raw, 1.0, 1.0, ALU.mult, ALU.mult)
                        else:
                            last = nc.gpsimd.tensor_tensor(lo, raw, f(hi), ALU.subtract)
                last.then_inc(s_uqh if part == 0 else s_uq, 1)
                if part == 0:
                    pool.wait_ge(s_uqh, 1)
            pool.wait_ge(s_ukvi, 16)
            for part in range(2):
                for k in range(KVLT):
                    for hi, lo, c in ((uk_hi, uk_lo, 0), (uv_hi, uv_lo, HD)):
                        raw = ukv_raw[:, k, :, c:c + HD]
                        if part == 0:
                            last = nc.gpsimd.tensor_scalar(hi[:, k, :, :], raw, 1.0, 1.0, ALU.mult, ALU.mult)
                        else:
                            last = nc.gpsimd.tensor_tensor(lo[:, k, :, :], raw, f(hi[:, k, :, :]), ALU.subtract)
                last.then_inc(s_ukvh if part == 0 else s_ukv, 1)
                if part == 0:
                    pool.wait_ge(s_ukvh, 1)

            def split_w(m):
                pool.wait_ge(s_w[m % 2], 16 * (m // 2 + 1))
                if m < 2:
                    pool.wait_ge(s_up, N_Q)
                else:
                    pool.wait_ge(s_g, 2 * (m - 1))
                split(w_raw[:, m % 2, :, :], w_hi[:, m % 2, :, :], w_lo[:, m % 2, :, :], s_wh, m + 1, s_wr)

            def probs_w(u):
                pool.wait_ge(s_wrd, u + 1)
                w = len(w_keys(u)) * P
                for r in range(REP):
                    nc.gpsimd.tensor_scalar(p_w[:, u % 2, r, 0:w], p_w[:, u % 2, r, 0:w], w_col(5, u)[:, r:r + 1],
                                            0.5, ALU.mult, ALU.mult).then_inc(s_wp, 1)

            def gate_w(u):
                n, g = u // GROUPS, u % GROUPS
                if u == 0:
                    pool.wait_ge(s_ge, N_WIN_JOB)
                pool.wait_ge(s_wo, u + 1)
                y = Y[:, 2 * g:2 * g + 2, n * P:(n + 1) * P]
                nc.gpsimd.tensor_tensor(y, y, o_w[:, u % 2, :, :], ALU.mult).then_inc(s_wy, 1)

            for m in range(NM - 2):
                split_w(m)
            for s in range(W_UNITS + 2):
                if s < W_UNITS:
                    probs_w(s)
                if s >= 2:
                    gate_w(s - 2)
                if s == 4:
                    split_w(NM - 2)
                if s == 8:
                    split_w(NM - 1)

            def split_head(h):
                hp = h % 2
                pool.wait_ge(s_qki, 64 * (h + 1))
                if h == 0:
                    pool.wait_ge(s_krl, 16)
                    pool.wait_ge(s_vr, 16)
                if h >= 2:
                    pool.wait_ge(s_bs, NT * (h - 1))
                split(q_raw[:, :], q_hi[:, hp, :], q_lo[:, hp, :], s_sph, 2 * h + 1, None)
                split(k_raw[:, :], k_hi[:, hp, :], k_lo[:, hp, :], s_sph, 2 * h + 2, s_sp)

            def split_v(h):
                hp = h % 2
                if h >= 2:
                    pool.wait_ge(s_bpv, 2 * (h - 1))
                raw = v_raw[:, :, h * HD:(h + 1) * HD]
                split(raw, vB[:, hp, :, 0:HD], vB[:, hp, :, HD:P], s_sph2, h + 1, s_sp2)

            def probs_b(U):
                pool.wait_ge(s_br, U + 1)
                nc.gpsimd.tensor_scalar(p_b[:, U % 3, :], p_b[:, U % 3, :], r_b[:, U % 4:U % 4 + 1], 0.5,
                                        ALU.mult, ALU.mult).then_inc(s_bp, 1)

            def gate_b(j, c):
                pool.wait_ge(s_bo, 4 * j + c + 3)
                y = Y[:, 4 + j, c * HALF:(c + 1) * HALF]
                nc.gpsimd.tensor_tensor(y, y, o_b[:, c, :], ALU.mult).then_inc(s_by, 1)

            pool.wait_ge(s_ge, 2 * NM)
            split_head(0)
            split_v(0)
            for U in range(B_UNITS + 8):
                if U < B_UNITS:
                    probs_b(U)
                if U % NT == 2 and U // NT + 1 < HEADS:
                    split_head(U // NT + 1)
                if U % NT == NT - 1 and U // NT + 1 < HEADS:
                    split_v(U // NT + 1)
                G = (U - 10) // 4
                if U >= 10 and (U - 10) % 4 == 0 and G % 4 >= 2:
                    gate_b(G // 4, G % 2)

            pool.wait_ge(s_bpv, B_GROUPS)
            for k in range(KT):
                pool.wait_ge(s_woi[k % 4], 16 * (k // 4 + 1))
                nc.gpsimd.tensor_scalar(wo_hi[:, k, :], wo_raw[:, k % 4, :], 1.0, 1.0, ALU.mult, ALU.mult) \
                    .then_inc(s_woh, 1)

        @block.scalar
        def _(act):
            def h_hi(t):
                act.wait_ge(s_xT, t + 1)
                b = 2 * (t % 2)
                nc.scalar.activation(hT_hi[:, :, t * P:(t + 1) * P],
                                     ps[:, b:b + 2, :].rearrange("p b (k c) -> p (b k) c", c=P),
                                     ACT.Copy).then_inc(s_hhi, 1)

            for t in range(NT):
                act.wait_ge(s_x[t % 2], 16 * (t // 2 + 1))
                if t >= 2:
                    act.wait_ge(s_xT, t - 1)
                nc.scalar.activation(x_n[:, t % 2, :], x_in[:, t % 2, :], ACT.Square,
                                     accum_out=ssq[:, t:t + 1]).then_inc(s_ssq, 1)
                if t >= 1:
                    h_hi(t - 1)
                act.wait_ge(s_var, t + 1)
                nc.scalar.activation(rms[:, t:t + 1], var[:, t:t + 1], ACT.Sqrt).then_inc(s_rms, 1)
            h_hi(NT - 1)

            def lat_hi(t):
                act.wait_ge(s_lT, t + 1)
                b = 2 * (t % 2)
                nc.scalar.activation(latT_hi[:, 0:4, t * P:(t + 1) * P],
                                     ps[:, b, :].rearrange("p (k c) -> p k c", c=P), ACT.Copy)
                nc.scalar.activation(latT_hi[:, 4, t * P:(t + 1) * P], ps[:, b + 1, 0:P],
                                     ACT.Copy).then_inc(s_lhi, 1)

            for t in range(NT):
                a, b = 4 + 2 * (t % 2), 5 + 2 * (t % 2)
                act.wait_ge(s_pA, t + 1)
                nc.scalar.activation(vA[:, t, :, 0:HD], ps[:, a, 0:P].rearrange("p (g c) -> p g c", c=HD),
                                     ACT.Copy)
                if t >= 2:
                    act.wait_ge(s_lT, t - 1)
                nc.scalar.activation(lat[:, t % 2, QL:QL + KVL], ps[:, a, P:P + KVL], ACT.Square,
                                     accum_out=lss[:, 1:2])
                nc.scalar.activation(kr_n[:, t, :], ps[:, a, P + KVL:NA], ACT.Copy).then_inc(s_va, 1)
                act.wait_ge(s_pB, t + 1)
                nc.scalar.activation(lat[:, t % 2, 0:QL], ps[:, b, 0:QL], ACT.Square,
                                     accum_out=lss[:, 0:1]).then_inc(s_lss, 1)
                if t >= 1:
                    lat_hi(t - 1)
                act.wait_ge(s_lvar, t + 1)
                nc.scalar.activation(lrms, lvar, ACT.Sqrt).then_inc(s_lrms, 1)
            lat_hi(NT - 1)

            for j, (kind, t, h) in enumerate(UP):
                if kind in BY_DVE:
                    continue
                act.wait_ge(s_up, j + 1)
                if j >= 4:
                    act.wait_ge(s_st[j % 4], 16 * (j // 4))
                n = ROPE if kind == "kr" else P
                if kind == "q":
                    nc.scalar.activation(stage[:, j % 4, :], ps[:, 4 + j % 4, :], ACT.Copy,
                                         scale=B_SCALE).then_inc(s_upa, 1)
                else:
                    nc.scalar.activation(stage[0:n, j % 4, :], ps[0:n, 4 + j % 4, :],
                                         ACT.Copy).then_inc(s_upa, 1)

            def evac_g(g):
                m, cols, bank = g // 2, slice(g % 2 * HALF, (g % 2 + 1) * HALF), g_bank(g)
                act.wait_ge(s_g, g + 1)
                if m == 0:
                    wait_all_stored(act)
                    for q in range(GROUPS):
                        for half in (0, HD):
                            last = nc.scalar.activation(k_hi2[half:half + HD, q, cols],
                                                        ps[HD * q:HD * (q + 1), bank, :], ACT.Copy)
                elif m < 5:
                    for q in range(2):
                        h = 2 * (m - 1) + q
                        last = nc.scalar.activation(q_st[0:HD, h, cols], ps[HD * q:HD * (q + 1), bank, :],
                                                    ACT.Copy, scale=A_SCALE / SLOPE[h])
                else:
                    last = nc.scalar.activation(Y[:, m - 5, cols], ps[:, bank, :], ACT.Tanh, scale=0.5)
                last.then_inc(s_ga, 1)

            def exp_w(u):
                w = len(w_keys(u)) * P
                act.wait_ge(s_wnm, u + 1)
                for r in range(REP):
                    p = p_w[:, u % 2, r, 0:w]
                    nc.scalar.activation(p, p, ACT.Exp, bias=w_col(1, u)[:, r:r + 1],
                                         accum_out=w_col(3, u)[:, r:r + 1])
                nc.scalar.activation(w_col(4, u), w_col(2, u), ACT.Exp).then_inc(s_we, 1)

            def pT_w_hi(c):
                act.wait_ge(s_wT, c + 1)
                if c >= 2:
                    act.wait_ge(s_wpv, c - 1)
                nc.scalar.activation(pT_wh[:, c % 2, :], ps[:, 4 + c % 2, :], ACT.Copy).then_inc(s_wTh, 1)

            def o_w_lo(u):
                act.wait_ge(s_wpv, W_FIRST[u + 1])
                if u >= 1:
                    act.wait_ge(s_wo, u)
                nc.scalar.activation(ol_w[:, :], ps[HD:P, 7, :], ACT.Copy).then_inc(s_wol, 1)

            for g in range(N_WIN_JOB):
                evac_g(g)
            for s in range(W_UNITS + 1):
                keys = range(W_FIRST[s - 1], W_FIRST[s]) if s >= 1 else []
                for c in keys[:2]:
                    pT_w_hi(c)
                if s < W_UNITS:
                    exp_w(s)
                for c in keys[2:]:
                    pT_w_hi(c)
                if s >= 1:
                    o_w_lo(s - 1)
                if s % 2 == 1:
                    evac_g(N_WIN_JOB + s // 2)

            def exp_b(U):
                act.wait_ge(s_bm, U + 1)
                if U >= 3:
                    act.wait_ge(s_bT, 2 * (U - 2))
                b = 2 * (U % 2)
                nc.scalar.activation(p_b[:, U % 3, :], ps[:, b:b + 2, :].rearrange("p b c -> p (b c)"), ACT.Exp,
                                     bias=nm_b[:, U % 4:U % 4 + 1],
                                     accum_out=sum_b[:, U % 4:U % 4 + 1]).then_inc(s_be, 1)

            def pT_b_hi(U, a):
                act.wait_ge(s_bT, 2 * U + a + 1)
                G = U // 4
                if U % 4 == 0 and a == 0 and G >= 2:
                    act.wait_ge(s_bpv, G - 1)
                nc.scalar.activation(pT_hi[:, G % 2, 4 * a:4 * a + 4, U % 4 * P:(U % 4 + 1) * P],
                                     ps[:, 4 + a, :].rearrange("p (k c) -> p k c", c=P),
                                     ACT.Copy).then_inc(s_bTh, 1)

            def o_b_lo(G):
                act.wait_ge(s_bpv, G + 1)
                if G >= 1:
                    act.wait_ge(s_bo, G)
                nc.scalar.activation(ol_b[:, :], ps[HD:P, 6 + G % 2, :], ACT.Copy).then_inc(s_bol, 1)

            for U in range(B_UNITS + 7):
                if 2 <= U < B_UNITS + 2:
                    pT_b_hi(U - 2, 0)
                    pT_b_hi(U - 2, 1)
                if U < B_UNITS:
                    exp_b(U)
                if U >= 9 and (U - 9) % 4 == 0:
                    o_b_lo((U - 9) // 4)

            for k in range(KT):
                if k == 0:
                    act.wait_ge(s_sp, HEADS)
                    act.wait_ge(s_bs, B_UNITS)
                    act.wait_ge(s_by, B_GROUPS // 2)
                nc.scalar.activation(y_hi[:, k, :], Y[:, k, :], ACT.Copy).then_inc(s_yh, 1)
            for t in range(NT):
                act.wait_ge(s_oadd, t + 1)
                nc.scalar.activation(x_r[:, t % 2, :], o_n[:, t % 2, :], ACT.Square,
                                     accum_out=ssq[:, t:t + 1]).then_inc(s_oss, 1)
                act.wait_ge(s_ovar, t + 1)
                nc.scalar.activation(rms[:, t:t + 1], var[:, t:t + 1], ACT.Sqrt).then_inc(s_orms, 1)

        @block.vector
        def _(dve):
            chain = [0]

            def link(ins):
                chain[0] += 1
                ins.then_inc(s_chain, 1)
                dve.wait_ge(s_chain, chain[0])

            def h_lo(t):
                dve.wait_ge(s_hhi, t + 1)
                b = 2 * (t % 2)
                hi = hT_hi[:, :, t * P:(t + 1) * P]
                nc.vector.tensor_tensor(hT_lo[:, :, t * P:(t + 1) * P],
                                        ps[:, b:b + 2, :].rearrange("p b (k c) -> p (b k) c", c=P),
                                        f(hi), ALU.subtract).then_inc(s_hT, 1)

            dve.wait_ge(s_gmix, 16)
            for t in range(NT):
                dve.wait_ge(s_ssq, t + 1)
                nc.vector.tensor_scalar(var[:, t:t + 1], ssq[:, t:t + 1], 1.0 / D, EPS, ALU.mult,
                                        ALU.add).then_inc(s_var, 1)
                if t >= 1:
                    h_lo(t - 1)
                dve.wait_ge(s_rms, t + 1)
                link(nc.vector.reciprocal(rstd[:, t:t + 1], rms[:, t:t + 1]))
                nc.vector.scalar_tensor_tensor(out=x_n[:, t % 2, :], in0=x_in[:, t % 2, :],
                                               scalar=rstd[:, t:t + 1], in1=g_mix[:, :], op0=ALU.mult,
                                               op1=ALU.mult).then_inc(s_xn, 1)
            h_lo(NT - 1)

            def lat_lo(t):
                dve.wait_ge(s_lhi, t + 1)
                b, cols = 2 * (t % 2), slice(t * P, (t + 1) * P)
                nc.vector.tensor_tensor(latT_lo[:, 0:4, cols], ps[:, b, :].rearrange("p (k c) -> p k c", c=P),
                                        f(latT_hi[:, 0:4, cols]), ALU.subtract)
                nc.vector.tensor_tensor(latT_lo[:, 4, cols], ps[:, b + 1, 0:P], f(latT_hi[:, 4, cols]),
                                        ALU.subtract).then_inc(s_latT, 1)

            dve.wait_ge(s_glat, 32)
            for t in range(NT):
                a, b = 4 + 2 * (t % 2), 5 + 2 * (t % 2)
                dve.wait_ge(s_va, t + 1)
                nc.vector.tensor_tensor(vA[:, t, :, HD:P], ps[:, a, 0:P].rearrange("p (g c) -> p g c", c=HD),
                                        f(vA[:, t, :, 0:HD]), ALU.subtract)
                dve.wait_ge(s_lss, t + 1)
                nc.vector.tensor_scalar(lvar[:, 0:1], lss[:, 0:1], 1.0 / QL, EPS, ALU.mult, ALU.add)
                nc.vector.tensor_scalar(lvar[:, 1:2], lss[:, 1:2], 1.0 / KVL, EPS, ALU.mult,
                                        ALU.add).then_inc(s_lvar, 1)
                if t >= 1:
                    lat_lo(t - 1)
                dve.wait_ge(s_lrms, t + 1)
                link(nc.vector.reciprocal(lrstd, lrms))
                nc.vector.scalar_tensor_tensor(out=lat[:, t % 2, 0:QL], in0=ps[:, b, 0:QL],
                                               scalar=lrstd[:, 0:1], in1=g_lat[:, 0:QL], op0=ALU.mult,
                                               op1=ALU.mult)
                nc.vector.scalar_tensor_tensor(out=lat[:, t % 2, QL:QL + KVL], in0=ps[:, a, P:P + KVL],
                                               scalar=lrstd[:, 1:2], in1=g_lat[:, QL:QL + KVL],
                                               op0=ALU.mult, op1=ALU.mult).then_inc(s_lat, 1)
            dve.wait_ge(s_rnat, 16)
            x1, x2, cos, sin = kr_n[:, :, 0:HR], kr_n[:, :, HR:ROPE], r_nat[:, 0, :, :], r_nat[:, 1, :, :]
            for i, (a, b) in enumerate(((x1, cos), (x2, sin), (x1, sin), (x2, cos))):
                last = nc.vector.tensor_tensor(kr_t[:, i, :, :], a, b, ALU.mult)
            link(last)
            nc.vector.tensor_tensor(kr_r[:, :, 0:HR], kr_t[:, 0, :, :], kr_t[:, 1, :, :], ALU.subtract)
            nc.vector.tensor_tensor(kr_r[:, :, HR:ROPE], kr_t[:, 2, :, :], kr_t[:, 3, :, :],
                                    ALU.add).then_inc(s_krr, 1)
            lat_lo(NT - 1)

            dve.wait_ge(s_rq, 16)
            for j, (kind, t, h) in enumerate(UP):
                if kind == "r" and t == 1:
                    x1, x2 = ps[:, 4 + (j - 1) % 4, :], ps[:, 4 + j % 4, :]
                    cos, sin = (r_q[:, i, h * HALF:(h + 1) * HALF] for i in range(2))
                    dve.wait_ge(s_up, j + 1)
                    if j > 1:
                        dve.wait_ge(s_upd, j - 1)
                    for i, (a, b) in enumerate(((x1, cos), (x2, sin), (x1, sin), (x2, cos))):
                        last = nc.vector.tensor_tensor(r_tmp[:, i, :], a, b, ALU.mult)
                    link(last)
                    nc.vector.tensor_tensor(stage[:, (j - 1) % 4, :], r_tmp[:, 0, :], r_tmp[:, 1, :],
                                            ALU.subtract)
                    nc.vector.tensor_tensor(stage[:, j % 4, :], r_tmp[:, 2, :], r_tmp[:, 3, :],
                                            ALU.add).then_inc(s_upd, 2)
                if kind == "v":
                    dve.wait_ge(s_up, j + 1)
                    dve.wait_ge(s_st[j % 4], 16 * (j // 4))
                    nc.vector.tensor_copy(stage[:, j % 4, :], ps[:, 4 + j % 4, :]).then_inc(s_upd, 1)

            def evac_g(g):
                m, cols, bank = g // 2, slice(g % 2 * HALF, (g % 2 + 1) * HALF), g_bank(g)
                dve.wait_ge(s_ga, g + 1)
                if m == 0:
                    for q in range(GROUPS):
                        for half in (0, HD):
                            last = nc.vector.tensor_tensor(k_lo2[half:half + HD, q, cols],
                                                           ps[HD * q:HD * (q + 1), bank, :],
                                                           f(k_hi2[half:half + HD, q, cols]), ALU.subtract)
                elif m < 5:
                    for q in range(2):
                        h = 2 * (m - 1) + q
                        last = nc.vector.scalar_tensor_tensor(
                            out=q_st[HD:P, h, cols], in0=ps[HD * q:HD * (q + 1), bank, :],
                            scalar=A_SCALE / SLOPE[h], in1=f(q_st[0:HD, h, cols]), op0=ALU.mult,
                            op1=ALU.subtract)
                else:
                    last = nc.vector.scalar_tensor_tensor(out=Y[:, m - 5, cols], in0=Y[:, m - 5, cols],
                                                          scalar=1.0, in1=ps[:, bank, :], op0=ALU.add,
                                                          op1=ALU.mult)
                last.then_inc(s_ge, 1)

            def max_w(u):
                n, g, keys = u // GROUPS, u % GROUPS, w_keys(u)
                c0, w = (keys[0] - (n - 1)) * P, len(keys) * P
                if u >= 2:
                    dve.wait_ge(s_wT, W_FIRST[u - 1])
                for r in range(REP):
                    h = REP * g + r
                    dve.wait_ge(s_ws, REP * u + r + 1)
                    nc.vector.tensor_tensor_reduce(out=p_w[:, u % 2, r, 0:w], in0=distb[:, c0:c0 + w],
                                                   in1=ps[:, r, 0:w], scale=SLOPE[h],
                                                   scalar=sinkb[:, h:h + 1], op0=ALU.add, op1=ALU.max,
                                                   accum_out=w_col(0, u)[:, r:r + 1]).then_inc(s_wm, 1)
                dve.wait_ge(s_wm, REP * (u + 1))
                nc.vector.tensor_scalar(w_col(1, u), w_col(0, u), -1.0, None, ALU.mult)
                nc.vector.tensor_tensor(w_col(2, u), sinkb[:, REP * g:REP * (g + 1)], w_col(0, u),
                                        ALU.subtract).then_inc(s_wnm, 1)

            def recip_w(u):
                dve.wait_ge(s_we, u + 1)
                link(nc.vector.tensor_tensor(w_col(4, u), w_col(3, u), w_col(4, u), ALU.add))
                nc.vector.reciprocal(w_col(5, u), w_col(4, u)).then_inc(s_wrd, 1)

            def pT_w_lo(c):
                dve.wait_ge(s_wTh, c + 1)
                nc.vector.tensor_tensor(pT_wl[:, c % 2, :], ps[:, 4 + c % 2, :], f(pT_wh[:, c % 2, :]),
                                        ALU.subtract).then_inc(s_wTl, 1)

            def o_w_sum(u):
                dve.wait_ge(s_wol, u + 1)
                if u >= 2:
                    dve.wait_ge(s_wy, u - 1)
                for q in range(2):
                    src = ps[0:HD, 7, :].rearrange("p (a b c) -> p a b c", b=2, c=P)[:, :, q, :]
                    low = ol_w[:, :].rearrange("p (a b c) -> p a b c", b=2, c=P)[:, :, q, :]
                    last = nc.vector.tensor_tensor(o_w[HD * q:HD * (q + 1), u % 2, :, :], src, low, ALU.add)
                last.then_inc(s_wo, 1)

            for g in range(N_WIN_JOB):
                evac_g(g)
            dve.wait_ge(s_dist, 16)
            dve.wait_ge(s_sink, 16)
            for s in range(W_UNITS + 1):
                keys = range(W_FIRST[s - 1], W_FIRST[s]) if s >= 1 else []
                if s < W_UNITS:
                    max_w(s)
                for c in keys:
                    pT_w_lo(c)
                if s < W_UNITS:
                    recip_w(s)
                if s >= 1:
                    o_w_sum(s - 1)
                if s % 2 == 1:
                    evac_g(N_WIN_JOB + s // 2)

            def max_b(U):
                dve.wait_ge(s_bs, U + 1)
                b = 2 * (U % 2)
                nc.vector.tensor_reduce(nm_b[:, U % 4:U % 4 + 1], ps[:, b:b + 2, :].rearrange("p b c -> p (b c)"),
                                        AX.X, ALU.max, negate=True).then_inc(s_bm, 1)

            def recip_b(U):
                dve.wait_ge(s_be, U + 1)
                nc.vector.reciprocal(r_b[:, U % 4:U % 4 + 1], sum_b[:, U % 4:U % 4 + 1]).then_inc(s_br, 1)

            def pT_b_lo(U, a):
                dve.wait_ge(s_bTh, 2 * U + a + 1)
                at_ = (slice(None), U // 4 % 2, slice(4 * a, 4 * a + 4), slice(U % 4 * P, (U % 4 + 1) * P))
                nc.vector.tensor_tensor(pT_lo[at_], ps[:, 4 + a, :].rearrange("p (k c) -> p k c", c=P),
                                        f(pT_hi[at_]), ALU.subtract).then_inc(s_bTl, 1)

            def o_b_sum(G):
                q = HD * (G // 2 % 2)
                dve.wait_ge(s_bol, G + 1)
                if G % 4 < 2 and G >= 4:
                    dve.wait_ge(s_by, 2 * (G // 4 - 1) + G % 2 + 1)
                nc.vector.tensor_tensor(o_b[q:q + HD, G % 2, :], ps[0:HD, 6 + G % 2, :], ol_b[:, :],
                                        ALU.add).then_inc(s_bo, 1)

            for U in range(B_UNITS + 7):
                if 1 <= U <= B_UNITS:
                    recip_b(U - 1)
                if U < B_UNITS:
                    max_b(U)
                if 2 <= U < B_UNITS + 2:
                    pT_b_lo(U - 2, 0)
                    pT_b_lo(U - 2, 1)
                if U >= 9 and (U - 9) % 4 == 0:
                    o_b_sum((U - 9) // 4)

            for k in range(KT):
                dve.wait_ge(s_yh, k + 1)
                nc.vector.tensor_tensor(y_lo[:, k, :], Y[:, k, :], f(y_hi[:, k, :]), ALU.subtract).then_inc(s_yl, 1)
                dve.wait_ge(s_woh, k + 1)
                nc.vector.tensor_tensor(wo_lo[:, k, :], wo_raw[:, k % 4, :], f(wo_hi[:, k, :]),
                                        ALU.subtract).then_inc(s_wol2, 1)
            dve.wait_ge(s_gfin, 16)
            for t in range(NT):
                b = 2 * (t % 4)
                dve.wait_ge(s_op, t + 1)
                dve.wait_ge(s_xr[t % 2], 16 * (t // 2 + 1))
                if t >= 2:
                    dve.wait_ge(s_out[t % 2], 16 * (t // 2))
                nc.vector.tensor_tensor(o_n[:, t % 2, :], ps[:, b:b + 2, :].rearrange("p b c -> p (b c)"),
                                        x_r[:, t % 2, :], ALU.add).then_inc(s_oadd, 1)
                dve.wait_ge(s_oss, t + 1)
                nc.vector.tensor_scalar(var[:, t:t + 1], ssq[:, t:t + 1], 1.0 / D, EPS, ALU.mult,
                                        ALU.add).then_inc(s_ovar, 1)
                dve.wait_ge(s_orms, t + 1)
                link(nc.vector.reciprocal(rstd[:, t:t + 1], rms[:, t:t + 1]))
                nc.vector.scalar_tensor_tensor(out=o_n[:, t % 2, :], in0=o_n[:, t % 2, :],
                                               scalar=rstd[:, t:t + 1], in1=g_fin[:, :], op0=ALU.mult,
                                               op1=ALU.mult).then_inc(s_on, 1)

        @block.tensor
        def _(pe):
            def three(o, a_hi, a_lo, b_hi, b_lo, first, last):
                nc.tensor.matmul(o, a_hi, b_hi, start=first, stop=False)
                nc.tensor.matmul(o, a_hi, b_lo, start=False, stop=False)
                return nc.tensor.matmul(o, a_lo, b_hi, start=False, stop=last)

            pe.wait_ge(s_id, 2)
            for t in range(NT):
                pe.wait_ge(s_xn, t + 1)
                if t >= 2:
                    pe.wait_ge(s_hT, t - 1)
                for k in range(KT):
                    last = nc.tensor.transpose(ps[:, 2 * (t % 2) + k // 4, k % 4 * P:(k % 4 + 1) * P],
                                               x_n[:, t % 2, k * P:(k + 1) * P], ident[:, :])
                last.then_inc(s_xT, 1)

            def turn_lat(t):
                pe.wait_ge(s_lat, t + 1)
                if t < 2:
                    pe.wait_ge(s_hT, NT)
                else:
                    pe.wait_ge(s_latT, t - 1)
                for k in range(LT):
                    last = nc.tensor.transpose(ps[:, 2 * (t % 2) + k // 4, k % 4 * P:(k % 4 + 1) * P],
                                               lat[:, t % 2, k * P:(k + 1) * P], ident[:, :])
                last.then_inc(s_lT, 1)

            for t in range(NT):
                cols = slice(t * P, (t + 1) * P)
                pe.wait_ge(s_hT, t + 1)
                if t >= 2:
                    pe.wait_ge(s_lat, t - 1)
                for c, w0, w1, done in ((0, 0, NA, s_pA), (1, NA, NW, s_pB)):
                    for k in range(KT):
                        if t == 0 and c == 0:
                            pe.wait_ge(s_wnr, k + 1)
                        last = three(ps[:, 4 + 2 * (t % 2) + c, 0:w1 - w0], hT_hi[:, k, cols], hT_lo[:, k, cols],
                                     wn_hi[:, k, w0:w1], wn_lo[:, k, w0:w1], k == 0, k == KT - 1)
                    last.then_inc(done, 1)
                if t >= 1:
                    turn_lat(t - 1)
            turn_lat(NT - 1)

            for j, (kind, t, h) in enumerate(UP):
                o = ps[:, 4 + j % 4, :]
                cols = slice(h * HALF, (h + 1) * HALF)
                if j == 0:
                    pe.wait_ge(s_latT, NT)
                    pe.wait_ge(s_uq, 1)
                if kind == "kr" and h == 0:
                    pe.wait_ge(s_krr, 1)
                if kind == "k" and t == 0 and h == 0:
                    pe.wait_ge(s_ukv, 1)
                if j >= 4:
                    wait_up_copied(pe, j - 4)
                if kind in ("r", "q"):
                    c = 4 + t if kind == "r" else t
                    for k in range(QLT):
                        last = three(o, uq_hi[:, k, c, :], uq_lo[:, k, c, :], latT_hi[:, k, cols],
                                     latT_lo[:, k, cols], k == 0, k == QLT - 1)
                elif kind == "kr":
                    for i in range(4):
                        last = nc.tensor.transpose(o[0:ROPE, i * P:(i + 1) * P], kr_r[:, 4 * h + i, :], ident[:, :])
                elif kind == "k":
                    for k in range(KVLT):
                        wh, wl = (a[:, k, 2 * t:2 * t + 2, :].rearrange("p a c -> p (a c)") for a in (uk_hi, uk_lo))
                        last = three(o, wh, wl, latT_hi[:, QLT + k, cols], latT_lo[:, QLT + k, cols],
                                     k == 0, k == KVLT - 1)
                else:
                    toks = slice(t * P, (t + 1) * P)
                    for k in range(KVLT):
                        wh, wl = (a[:, k, :, :].rearrange("p a c -> p (a c)") for a in (uv_hi, uv_lo))
                        last = three(o, latT_hi[:, QLT + k, toks], latT_lo[:, QLT + k, toks], wh, wl,
                                     k == 0, k == KVLT - 1)
                last.then_inc(s_up, 1)

            def gated(g, ks):
                m, cols = g // 2, slice(g % 2 * HALF, (g % 2 + 1) * HALF)
                if ks[0] == 0:
                    pe.wait_ge(s_wr, m + 1)
                    if g < 2:
                        wait_up_copied(pe, len(UP) - 2 + g)
                    else:
                        pe.wait_ge(s_ge, g if g > N_WIN_JOB else g - 1)
                for k in ks:
                    last = three(ps[:, g_bank(g), :], w_hi[:, m % 2, k, :], w_lo[:, m % 2, k, :],
                                 hT_hi[:, k, cols], hT_lo[:, k, cols], k == 0, k == KT - 1)
                if ks[-1] == KT - 1:
                    last.then_inc(s_g, 1)

            def scores_w(u):
                n, g, keys = u // GROUPS, u % GROUPS, w_keys(u)
                k0, w = keys[0] * P, len(keys) * P
                for r in range(REP):
                    if u >= 1:
                        pe.wait_ge(s_wm, REP * (u - 1) + r + 1)
                    q = q_st[:, REP * g + r, n * P:(n + 1) * P]
                    nc.tensor.matmul(ps[:, r, 0:w], q, k_hi2[:, g, k0:k0 + w], start=True, stop=False)
                    nc.tensor.matmul(ps[:, r, 0:w], q, k_lo2[:, g, k0:k0 + w], start=False,
                                     stop=True).then_inc(s_ws, 1)

            def turn_w(u, i):
                c = W_FIRST[u] + i
                if i == 0:
                    pe.wait_ge(s_wp, REP * (u + 1))
                if c >= 2:
                    pe.wait_ge(s_wTl, c - 1)
                elif c == 0:
                    wait_up_copied(pe, len(UP) - 4)
                    wait_up_copied(pe, len(UP) - 3)
                for r in range(REP):
                    last = nc.tensor.transpose(ps[:, 4 + c % 2, r * P:(r + 1) * P],
                                               p_w[:, u % 2, r, i * P:(i + 1) * P], ident[:, :])
                last.then_inc(s_wT, 1)

            def pv_w(u, i):
                c, keys = W_FIRST[u] + i, w_keys(u)
                if i == 0:
                    pe.wait_ge(s_wo, u) if u else pe.wait_ge(s_ge, N_WIN_JOB)
                pe.wait_ge(s_wTl, c + 1)
                v = vA[:, keys[i], u % GROUPS, :]
                nc.tensor.matmul(ps[:, 7, :], v, pT_wh[:, c % 2, :], start=(i == 0), stop=False)
                nc.tensor.matmul(ps[:, 7, :], v, pT_wl[:, c % 2, :], start=False,
                                 stop=(i == len(keys) - 1)).then_inc(s_wpv, 1)

            for g in range(N_WIN_JOB):
                gated(g, range(KT))
            for s in range(W_UNITS + 1):
                g, k0 = N_WIN_JOB + s // 2, 4 * (s % 2)
                n = len(w_keys(s - 1)) if s >= 1 else 0
                if s < W_UNITS:
                    scores_w(s)
                if n:
                    turn_w(s - 1, 0)
                    turn_w(s - 1, 1)
                if s < W_UNITS:
                    gated(g, range(k0, k0 + 2))
                if n:
                    pv_w(s - 1, 0)
                    if n > 2:
                        turn_w(s - 1, 2)
                if s < W_UNITS:
                    gated(g, range(k0 + 2, k0 + 4))
                for i in range(1, n):
                    pv_w(s - 1, i)

            def scores_b(U):
                h, t, hp = U // NT, U % NT, U // NT % 2
                if t == 0:
                    pe.wait_ge(s_sp, h + 1)
                if U >= 2:
                    pe.wait_ge(s_be, U - 1)
                q = slice(t * P, (t + 1) * P)
                for c in range(2):
                    k = slice(c * HALF, (c + 1) * HALF)
                    last = three(ps[:, 2 * (U % 2) + c, :], q_hi[:, hp, q], q_lo[:, hp, q], k_hi[:, hp, k],
                                 k_lo[:, hp, k], True, True)
                last.then_inc(s_bs, 1)

            def turn_b(U):
                pe.wait_ge(s_bp, U + 1)
                for a in range(2):
                    if U >= 1:
                        pe.wait_ge(s_bTl, 2 * (U - 1) + a + 1)
                    else:
                        pe.wait_ge(s_wTl, W_FIRST[W_UNITS])
                    for k in range(4):
                        last = nc.tensor.transpose(ps[:, 4 + a, k * P:(k + 1) * P],
                                                   p_b[:, U % 3, (4 * a + k) * P:(4 * a + k + 1) * P], ident[:, :])
                    last.then_inc(s_bT, 1)

            def pv_b(G, part):
                hp = G // 2 % 2
                if part == 0:
                    pe.wait_ge(s_sp2, G // 2 + 1)
                    pe.wait_ge(s_bTl, 8 * (G + 1))
                    if G >= 2:
                        pe.wait_ge(s_bo, G - 1)
                    else:
                        pe.wait_ge(s_wo, W_UNITS)
                        pe.wait_ge(s_ge, 2 * NM)
                for k in (2 * part, 2 * part + 1):
                    o = ps[:, 6 + G % 2, :]
                    nc.tensor.matmul(o, vB[:, hp, k, :], pT_hi[:, G % 2, k, :], start=(k == 0), stop=False)
                    last = nc.tensor.matmul(o, vB[:, hp, k, :], pT_lo[:, G % 2, k, :], start=False,
                                            stop=(k == NT - 1))
                if part == 3:
                    last.then_inc(s_bpv, 1)

            pe.wait_ge(s_wm, REP * W_UNITS)
            for U in range(B_UNITS + 6):
                if U < B_UNITS:
                    scores_b(U)
                if 2 <= U < B_UNITS + 2:
                    turn_b(U - 2)
                if U >= 6:
                    pv_b((U - 6) // 4, (U - 6) % 4)

            for t0 in range(0, NT, 4):
                order = [(k, t) for k in range(KT) for t in range(t0, t0 + 4)] if t0 == 0 else \
                    [(k, t) for t in range(t0, t0 + 4) for k in range(KT)]
                for k, t in order:
                    if t0 == 0 and t == 0:
                        pe.wait_ge(s_yl, k + 1)
                        pe.wait_ge(s_wol2, k + 1)
                        if k == 0:
                            pe.wait_ge(s_be, B_UNITS)
                            pe.wait_ge(s_bTl, 2 * B_UNITS)
                            pe.wait_ge(s_bo, B_GROUPS)
                    if t0 and k == 0:
                        pe.wait_ge(s_oadd, t - 3)
                    for c in range(2):
                        last = three(ps[:, 2 * (t % 4) + c, :], y_hi[:, k, t * P:(t + 1) * P],
                                     y_lo[:, k, t * P:(t + 1) * P], wo_hi[:, k, c * HALF:(c + 1) * HALF],
                                     wo_lo[:, k, c * HALF:(c + 1) * HALF], k == 0, k == KT - 1)
                    if k == KT - 1:
                        last.then_inc(s_op, 1)


def _constants():
    pos = np.arange(SEQ, dtype=np.float32)
    inv = np.float32(10000.0) ** (-np.arange(0, ROPE, 2, dtype=np.float32) / np.float32(ROPE))
    ang = pos[:, None] * inv[None, :]
    cs = np.stack([np.cos(ang), np.sin(ang)]).astype(np.float32)
    nat = cs.reshape(2, NT, P, HR).transpose(2, 0, 1, 3)
    q = np.tile(cs.transpose(0, 2, 1), (1, HEADS, 1)).transpose(1, 0, 2)
    q = q.astype(np.float64) * B_SCALE
    away = np.abs(np.arange(P)[:, None] - np.arange(3 * P)[None, :] + P)
    dist = np.where(away <= P, -away.astype(np.float32), np.float32(MASKED))
    return {"rope_nat": nat.astype(np.float32), "rope_q": q.astype(np.float32),
            "dist": dist.astype(np.float32)}


_INS = ["x", "norm_mix", "w_in", "attn_sink", "q_a_norm", "w_uq", "kv_a_norm", "w_ukv", "w_out", "final_norm"]


def kernel(**inputs):
    import concourse.bacc as _bacc
    from concourse.bass_utils import run_bass_kernel_spmd as _run

    nc = _bacc.Bacc("TRN2", target_bir_lowering=False, num_devices=1)
    arrays, args = {}, {}
    for name in _INS:
        a = np.ascontiguousarray(inputs[name])
        if name != "final_norm":
            a = a[0]
        arrays[name] = np.ascontiguousarray(a)
    for name, a in _constants().items():
        arrays[name] = np.ascontiguousarray(a)
    for name, a in arrays.items():
        args[name] = nc.dram_tensor(name, a.shape, mybir.dt.from_np(a.dtype), kind="ExternalInput").ap()
    out = nc.dram_tensor("out", (SEQ, D), F32, kind="ExternalOutput").ap()
    encoder(nc, out=out, **args)
    r = _run(nc, [arrays], core_ids=[0])
    return r.results[0]["out"].reshape(1, SEQ, D)
```

```python
from contextlib import ExitStack

import numpy as np

import concourse.bass as bass
from concourse import mybir

F32 = mybir.dt.float32
F32R = mybir.dt.float32r
ALU = mybir.AluOpType
ACT = mybir.ActivationFunctionType
AX = mybir.AxisListType

P = 128
SEQ = 1024
D = 1024
NT = SEQ // P
KT = D // P
HALF = 512
HEADS = 8
HD = 64
GROUPS = 2
REP = HEADS // GROUPS
ROPE = 32
HR = ROPE // 2
QK = HD + ROPE
QL = 384
KVL = 256
QLT = QL // P
KVLT = KVL // P
LT = QLT + KVLT
A_SCALE = HD ** -0.5
B_SCALE = QK ** -0.5
EPS = 1e-6
MASKED = 1e30

QA, KA, VA, GA, CQ = 0, 512, 640, 768, 1280
CKV = CQ + QL
KR = CKV + KVL
GB = KR + ROPE
NA = P + KVL + ROPE
NW = NA + QL

BASE = 16512
POOL_R = 3
SLOPE = [2.0 ** -(h + 1) for h in range(HEADS)]


def f(ap):
    return ap.bitcast(F32)


def encoder(nc, x, norm_mix, w_in, attn_sink, q_a_norm, w_uq, kv_a_norm, w_ukv, w_out, final_norm,
            rope_nat, rope_q, dist, out):
    q_scr = nc.dram_tensor("q_nope_scratch", [HEADS * HD, SEQ], F32, kind="Internal").ap()
    qr_scr = nc.dram_tensor("q_rope_scratch", [2, P, SEQ], F32, kind="Internal").ap()
    k_scr = nc.dram_tensor("k_nope_scratch", [HEADS * HD, SEQ], F32, kind="Internal").ap()
    kr_scr = nc.dram_tensor("k_rope_scratch", [ROPE, SEQ], F32, kind="Internal").ap()
    v_scr = nc.dram_tensor("v_scratch", [SEQ, HEADS * HD], F32, kind="Internal").ap()

    with ExitStack() as ctx:
        def sem(name):
            return ctx.enter_context(nc.semaphore(name))

        def at(name, kb, shape, dt=F32):
            return nc.alloc_sbuf_tensor_at(name, shape, dt, offset=BASE + int(kb * 1024))

        ident = at("ident", 0, [P, P])
        stat = at("stat", 0.5, [P, 96])
        sinkb = at("sinkb", 0.875, [P, HEADS])
        nsink = at("nsink", 0.90625, [P, HEADS])
        hT_hi = at("hT_hi", 1, [P, KT, SEQ], F32R)
        hT_lo = at("hT_lo", 33, [P, KT, SEQ], F32R)
        wn_hi = at("wn_hi", 65, [P, KT, NW], F32R)
        wn_lo = at("wn_lo", 90, [P, KT, NW], F32R)
        wn_raw = at("wn_raw", 115, [P, 3, NW])
        x_in = at("x_in", 124.5, [P, 2, D])
        x_n = at("x_n", 132.5, [P, 2, D])
        g_mix = at("g_mix", 140.5, [P, D])
        g_lat = at("g_lat", 144.5, [P, QL + KVL])
        lat = at("lat", 147, [P, 2, QL + KVL])
        kr_n = at("kr_n", 152, [P, NT, ROPE])
        kr_r = at("kr_r", 153, [P, NT, ROPE])
        kr_t = at("kr_t", 154, [P, 4, NT, HR])
        r_nat = at("r_nat", 156, [P, 2, NT, HR])
        vA = at("vA", 157, [P, NT, GROUPS, P], F32R)
        latT_hi = at("latT_hi", 165, [P, LT, SEQ], F32R)
        latT_lo = at("latT_lo", 185, [P, LT, SEQ], F32R)
        uq_raw = at("uq_raw", 115, [P, QLT, HEADS, QK])
        uq_hi = at("uq_hi", 124.5, [P, QLT, 6, P], F32R)
        uq_lo = at("uq_lo", 133.5, [P, QLT, 6, P], F32R)
        ukv_raw = at("ukv_raw", 65, [P, KVLT, HEADS, P])
        uk_hi = at("uk_hi", 73, [P, KVLT, HEADS, HD], F32R)
        uk_lo = at("uk_lo", 77, [P, KVLT, HEADS, HD], F32R)
        uv_hi = at("uv_hi", 81, [P, KVLT, HEADS, HD], F32R)
        uv_lo = at("uv_lo", 85, [P, KVLT, HEADS, HD], F32R)
        stage = at("stage", 89, [P, 4, HALF])
        r_tmp = at("r_tmp", 97, [P, 4, HALF])
        r_q = at("r_q", 105, [P, 2, SEQ])
        q_st = at("q_st", 65, [P, HEADS, SEQ], F32R)
        k_hi2 = at("k_hi2", 97, [P, GROUPS, SEQ], F32R)
        k_lo2 = at("k_lo2", 105, [P, GROUPS, SEQ], F32R)
        o_w = at("o_w", 113, [P, 2, 2, P])
        w_raw = at("w_raw", 115, [P, 2, KT, P])
        w_hi = at("w_hi", 124.5, [P, 2, KT, P], F32R)
        w_lo = at("w_lo", 132.5, [P, 2, KT, P], F32R)
        distb = at("distb", 140.5, [P, 3 * P])
        p_w = at("p_w", 142, [P, 2, REP, 3 * P])
        ol_w = at("ol_w", 154, [HD, HALF])
        pT_wh = at("pT_wh", 197, [P, 2, HALF], F32R)
        pT_wl = at("pT_wl", 201, [P, 2, HALF], F32R)
        Y = at("Y", 165, [P, KT, SEQ])
        pT_hi = at("pT_hi", 1, [P, 2, NT, HALF], F32R)
        pT_lo = at("pT_lo", 33, [P, 2, NT, HALF], F32R)
        q_hi = at("q_hi", 65, [QK, 2, SEQ], F32R)
        q_lo = at("q_lo", 73, [QK, 2, SEQ], F32R)
        k_hi = at("k_hi", 81, [QK, 2, SEQ], F32R)
        k_lo = at("k_lo", 89, [QK, 2, SEQ], F32R)
        v_raw = at("v_raw", 97, [P, NT, HEADS * HD])
        ol_b = at("ol_b", 113, [HD, HALF])
        q_raw = at("q_raw", 115, [QK, SEQ])
        k_raw = at("k_raw", 119, [QK, SEQ])
        vB = at("vB", 124.5, [P, 2, NT, P], F32R)
        p_b = at("p_b", 132.5, [P, 4, SEQ])
        wo_raw = at("wo_raw", 148.5, [P, 4, D])
        o_b = at("o_b", 197, [P, 2, HALF])
        wo_hi = at("wo_hi", 1, [P, KT, D], F32R)
        wo_lo = at("wo_lo", 33, [P, KT, D], F32R)
        y_hi = at("y_hi", 65, [P, KT, SEQ], F32R)
        y_lo = at("y_lo", 97, [P, KT, SEQ], F32R)
        x_r = at("x_r", 132.5, [P, 2, D])
        o_n = at("o_n", 140.5, [P, 2, D])
        g_fin = at("g_fin", 201, [P, D])

        ssq, var, rms, rstd = (stat[:, 8 * i:8 * i + 8] for i in range(4))
        lss, lvar, lrms, lrstd = (stat[:, 32 + 2 * i:34 + 2 * i] for i in range(4))

        def w_col(kind, u):
            c = 48 + 24 * (u % 2) + 4 * kind
            return stat[:, c:c + 4]

        nm_b, sum_b, r_b = (stat[:, 40 + 8 * 0 + 0:44], stat[:, 44:48], stat[:, 32:36])

        ps = ctx.enter_context(nc.psum_tensor("ps", [P, 8, HALF], F32))

        s_id = sem("ident_ready")
        s_gmix, s_glat, s_rnat, s_rq, s_sink, s_dist, s_gfin = (
            sem(n) for n in ("g_mix_in", "g_lat_in", "rope_nat_in", "rope_q_in", "sink_in", "dist_in",
                             "g_fin_in"))
        s_x = [sem(f"x_in{i}") for i in range(2)]
        s_wn = [sem(f"wn_in{i}") for i in range(3)]
        s_chain = sem("dve_chain")
        s_ssq, s_var, s_rms, s_xn = sem("ssq_ready"), sem("var_ready"), sem("rms_ready"), sem("xn_ready")
        s_xT, s_hhi, s_hT = sem("xT_done"), sem("hT_hi_ready"), sem("hT_ready")
        s_wnh, s_wnr = sem("wn_hi_ready"), sem("wn_ready")
        s_pA, s_pB = sem("natA_done"), sem("natB_done")
        s_va, s_lss, s_lvar, s_lrms, s_lat = (sem(n) for n in (
            "va_hi_ready", "lat_ssq_ready", "lat_var_ready", "lat_rms_ready", "lat_ready"))
        s_lT, s_lhi, s_latT = sem("lat_transposed"), sem("latT_hi_ready"), sem("latT_ready")
        s_krr = sem("k_rope_ready")
        s_uqi, s_ukvi = sem("uq_in"), sem("ukv_in")
        s_uqh, s_uq, s_ukvh, s_ukv = sem("uq_hi_ready"), sem("uq_ready"), sem("ukv_hi_ready"), sem("ukv_ready")
        s_up, s_upa, s_upd = sem("up_done"), sem("up_copied_act"), sem("up_copied_dve")
        s_st = [sem(f"stage_stored{i}") for i in range(4)]
        s_w = [sem(f"w_in{i}") for i in range(2)]
        s_wh, s_wr = sem("w_hi_ready"), sem("w_ready")
        s_g, s_ga, s_ge = sem("gated_done"), sem("gated_act"), sem("gated_evacuated")
        s_ws, s_wm, s_wnm, s_we, s_wrd, s_wp = (sem(n) for n in (
            "w_scores", "w_max", "w_negmax", "w_exp", "w_recip", "w_probs_pool"))
        s_wpd = sem("w_probs_dve")
        s_wT, s_wTh, s_wTl, s_wpv, s_wol, s_wo, s_wy = (sem(n) for n in (
            "w_transposed", "w_pT_hi", "w_pT_lo", "w_pv", "w_o_lo", "w_o", "w_y"))
        s_h0, s_h0l = sem("head0_hi"), sem("head0_split")
        s_vr, s_krl, s_qki = sem("v_raw_in"), sem("k_rope_in"), sem("qk_raw_in")
        s_sph, s_sph2, s_sp, s_sp2 = sem("qk_hi_split"), sem("v_hi_split"), sem("qk_split"), sem("v_split")
        s_bs, s_bm, s_be, s_br, s_bp = (sem(n) for n in (
            "b_scores", "b_negmax", "b_exp", "b_recip", "b_probs"))
        s_bT, s_bTh, s_bTl, s_bpv, s_bol, s_bo, s_by = (sem(n) for n in (
            "b_transposed", "b_pT_hi", "b_pT_lo", "b_pv", "b_o_lo", "b_o", "b_y"))
        s_woi = [sem(f"wo_in{i}") for i in range(4)]
        s_yh, s_yl, s_woh, s_wol2 = sem("y_hi_ready"), sem("y_ready"), sem("wo_hi_ready"), sem("wo_ready")
        s_xr = [sem(f"x_again{i}") for i in range(2)]
        s_op, s_oadd, s_oss, s_ovar, s_orms, s_on = (sem(n) for n in (
            "out_projected", "out_added", "out_ssq", "out_var", "out_rms", "out_normed"))
        s_out = [sem(f"out_stored{i}") for i in range(2)]

        UP = []
        for half in range(2):
            UP += [("q", j, half) for j in range(4)] + [("r", 0, half), ("r", 1, half), ("kr", 0, half)]
        UP += [("k", j, half) for j in range(4) for half in range(2)]
        UP += [("v", t, 0) for t in range(NT)]
        UP_BANK = (6, 7, 2, 3)
        BY_DVE = ("r", "v")
        N_Q = 13

        def wait_up_copied(eng, j):
            dve = UP[j][0] in BY_DVE
            n = sum(1 for k in UP[:j + 1] if (k[0] in BY_DVE) == dve)
            if UP[j][0] == "r" and UP[j][1] == 0:
                n += 1
            eng.wait_ge(s_upd if dve else s_upa, n)

        def wait_all_stored(eng):
            for i in range(4):
                eng.wait_ge(s_st[i], 16 * len(range(i, len(UP), 4)))

        M_COLS = [KA] + [QA + P * i for i in range(4)] + [GA + P * i for i in range(4)] \
            + [GB + P * i for i in range(4)]
        NM = len(M_COLS)
        N_WIN_JOB = 2 * (NM - 4)

        def g_bank(g):
            return 6 + g % 2 if g < N_WIN_JOB else 6

        def w_keys(u):
            n = u // GROUPS
            return range(max(n - 1, 0), min(n + 2, NT))

        W_UNITS = NT * GROUPS
        W_FIRST = [sum(len(w_keys(v)) for v in range(u)) for u in range(W_UNITS + 1)]

        B_UNITS = HEADS * NT
        B_GROUPS = B_UNITS // 4

        def nat_banks(t):
            return 2 + 2 * (t % 3), 3 + 2 * (t % 3)

        block = ctx.enter_context(nc.Block())

        @block.sync
        def _(sp):
            def load_x(t):
                if t >= 2:
                    sp.wait_ge(s_xn, t - 1)
                sp.dma_start(x_in[:, t % 2, :], x[t * P:(t + 1) * P, :]).then_inc(s_x[t % 2], 16)

            def load_wn(k):
                if k >= 3:
                    sp.wait_ge(s_wnr, k - 2)
                rows = w_in[k * P:(k + 1) * P, :]
                sp.dma_start(wn_raw[:, k % 3, 0:P], rows[:, VA:VA + P]).then_inc(s_wn[k % 3], 16)
                sp.dma_start(wn_raw[:, k % 3, P:NA], rows[:, CKV:CKV + KVL + ROPE]).then_inc(s_wn[k % 3], 16)
                sp.dma_start(wn_raw[:, k % 3, NA:NW], rows[:, CQ:CQ + QL]).then_inc(s_wn[k % 3], 16)

            load_x(0)
            sp.dma_start(g_mix[:, :], norm_mix.partition_broadcast(P)).then_inc(s_gmix, 16)
            load_wn(0)
            load_x(1)
            load_wn(1)
            load_x(2)
            load_wn(2)
            for t in range(3, NT):
                load_wn(t)
                load_x(t)
            sp.dma_start(g_lat[:, 0:QL], q_a_norm.partition_broadcast(P)).then_inc(s_glat, 16)
            sp.dma_start(g_lat[:, QL:QL + KVL], kv_a_norm.partition_broadcast(P)).then_inc(s_glat, 16)
            sp.dma_start(r_nat[:, :, :, :], rope_nat).then_inc(s_rnat, 16)
            sp.dma_start(sinkb[:, :], attn_sink.partition_broadcast(P)).then_inc(s_sink, 16)
            sp.wait_ge(s_wnr, KT)
            sp.dma_start(uq_raw[:, :, :, :],
                         w_uq.rearrange("(k p) (h c) -> p k h c", p=P, c=QK)).then_inc(s_uqi, 16)
            sp.wait_ge(s_pB, NT)
            sp.dma_start(ukv_raw[:, :, :, :],
                         w_ukv.rearrange("(k p) (h c) -> p k h c", p=P, c=P)).then_inc(s_ukvi, 16)
            sp.dma_start(r_q[:, :, :], rope_q).then_inc(s_rq, 16)

            def load_w(m):
                if m >= 2:
                    sp.wait_ge(s_wr, m - 1)
                elif m == 0:
                    sp.wait_ge(s_uq, 1)
                sp.dma_start(w_raw[:, m % 2, :, :],
                             w_in[:, M_COLS[m]:M_COLS[m] + P].rearrange("(k p) c -> p k c", p=P)) \
                    .then_inc(s_w[m % 2], 16)

            load_w(0)
            load_w(1)
            for j, (kind, t, h) in enumerate(UP):
                wait_up_copied(sp, j)
                src, cols = stage[:, j % 4, :], slice(h * HALF, (h + 1) * HALF)
                if kind == "r":
                    dst = qr_scr[t, :, cols]
                elif kind == "q":
                    dst = q_scr[t * P:(t + 1) * P, cols]
                elif kind == "kr":
                    dst, src = kr_scr[:, cols], stage[0:ROPE, j % 4, :]
                elif kind == "k":
                    dst = k_scr[t * P:(t + 1) * P, cols]
                else:
                    dst = v_scr[t * P:(t + 1) * P, :]
                sp.dma_start(dst, src).then_inc(s_st[j % 4], 16)
            sp.wait_ge(s_hT, 2 * NT)
            sp.dma_start(distb[:, :], dist).then_inc(s_dist, 16)
            for m in range(2, NM):
                load_w(m)

            wait_all_stored(sp)
            sp.wait_ge(s_wr, NM)
            sp.dma_start(k_raw[HD:QK, :], kr_scr).then_inc(s_krl, 16)

            def load_qk(h):
                if h >= 2:
                    sp.wait_ge(s_sp, 2 * (h - 1))
                elif h == 1:
                    sp.wait_ge(s_h0l, 1)
                sp.dma_start(q_raw[0:HD, :], q_scr[h * HD:(h + 1) * HD, :]).then_inc(s_qki, 16)
                for i in range(2):
                    sp.dma_start(q_raw[HD + i * HR:HD + (i + 1) * HR, :],
                                 qr_scr[i, h * HR:(h + 1) * HR, :]).then_inc(s_qki, 16)
                sp.dma_start(k_raw[0:HD, :], k_scr[h * HD:(h + 1) * HD, :]).then_inc(s_qki, 16)

            load_qk(0)
            sp.wait_ge(s_ws, REP * W_UNITS)
            sp.dma_start(v_raw[:, :, :], v_scr.rearrange("(t p) c -> p t c", p=P)).then_inc(s_vr, 16)
            for h in range(1, HEADS):
                load_qk(h)

            def load_wo(k):
                if k >= 4:
                    sp.wait_ge(s_wol2, k - 3)
                sp.dma_start(wo_raw[:, k % 4, :], w_out[k * P:(k + 1) * P, :]).then_inc(s_woi[k % 4], 16)

            sp.wait_ge(s_wT, W_FIRST[W_UNITS])
            sp.wait_ge(s_wo, W_UNITS)
            for k in range(4):
                load_wo(k)
            sp.dma_start(g_fin[:, :], final_norm.partition_broadcast(P)).then_inc(s_gfin, 16)

            def load_again(t):
                if t == 0:
                    sp.wait_ge(s_bT, 2 * B_UNITS)
                if t >= 2:
                    sp.wait_ge(s_oss, t - 1)
                sp.dma_start(x_r[:, t % 2, :], x[t * P:(t + 1) * P, :]).then_inc(s_xr[t % 2], 16)

            load_again(0)
            load_again(1)
            for k in range(4, KT):
                load_wo(k)
            for t in range(NT):
                sp.wait_ge(s_on, t + 1)
                sp.dma_start(out[t * P:(t + 1) * P, :], o_n[:, t % 2, :]).then_inc(s_out[t % 2], 16)
                if t + 2 < NT:
                    load_again(t + 2)
            for i in range(2):
                sp.wait_ge(s_out[i], 16 * NT // 2)

        @block.gpsimd
        def _(pool):
            def split(raw, hi, lo, done_hi, n_hi, done):
                nc.gpsimd.tensor_scalar(hi, raw, 1.0, 1.0, ALU.mult, ALU.mult).then_inc(done_hi, 1)
                pool.wait_ge(done_hi, n_hi)
                last = nc.gpsimd.tensor_tensor(lo, raw, f(hi), ALU.subtract)
                if done is not None:
                    last.then_inc(done, 1)
                return last

            nc.gpsimd.memset(ident[:, :], 0.0).then_inc(s_id, 1)
            pool.wait_ge(s_id, 1)
            nc.gpsimd.affine_select(out=ident[:, :], in_=ident[:, :], compare_op=ALU.not_equal, fill=1.0,
                                    base=0, pattern=[[-1, P]], channel_multiplier=1).then_inc(s_id, 1)
            for k in range(KT):
                pool.wait_ge(s_wn[k % 3], 48 * (k // 3 + 1))
                split(wn_raw[:, k % 3, :], wn_hi[:, k, :], wn_lo[:, k, :], s_wnh, k + 1, s_wnr)
            pool.wait_ge(s_uqi, 16)
            pool.wait_ge(s_xT, 2 * NT)
            for part in range(2):
                for k in range(QLT):
                    for dst, c, w in ((slice(0, 4), 0, HD), (4, HD, HR), (5, HD + HR, HR)):
                        hi, lo = uq_hi[:, k, dst, :], uq_lo[:, k, dst, :]
                        if w == HD:
                            hi, lo = (a.rearrange("p a (b c) -> p (a b) c", c=w) for a in (hi, lo))
                        else:
                            hi, lo = (a.rearrange("p (b c) -> p b c", c=w) for a in (hi, lo))
                        raw = uq_raw[:, k, :, c:c + w]
                        if part == 0:
                            last = nc.gpsimd.tensor_scalar(hi, raw, 1.0, 1.0, ALU.mult, ALU.mult)
                        else:
                            last = nc.gpsimd.tensor_tensor(lo, raw, f(hi), ALU.subtract)
                last.then_inc(s_uqh if part == 0 else s_uq, 1)
                if part == 0:
                    pool.wait_ge(s_uqh, 1)
            pool.wait_ge(s_ukvi, 16)
            for part in range(2):
                for k in range(KVLT):
                    for hi, lo, c in ((uk_hi, uk_lo, 0), (uv_hi, uv_lo, HD)):
                        raw = ukv_raw[:, k, :, c:c + HD]
                        if part == 0:
                            last = nc.gpsimd.tensor_scalar(hi[:, k, :, :], raw, 1.0, 1.0, ALU.mult, ALU.mult)
                        else:
                            last = nc.gpsimd.tensor_tensor(lo[:, k, :, :], raw, f(hi[:, k, :, :]), ALU.subtract)
                last.then_inc(s_ukvh if part == 0 else s_ukv, 1)
                if part == 0:
                    pool.wait_ge(s_ukvh, 1)

            def split_w(m):
                pool.wait_ge(s_w[m % 2], 16 * (m // 2 + 1))
                if m < 2:
                    pool.wait_ge(s_up, N_Q)
                else:
                    pool.wait_ge(s_g, 2 * (m - 1))
                split(w_raw[:, m % 2, :, :], w_hi[:, m % 2, :, :], w_lo[:, m % 2, :, :], s_wh, m + 1, s_wr)

            def probs_w(u):
                pool.wait_ge(s_wrd, u + 1)
                w = len(w_keys(u)) * P
                for r in range(POOL_R):
                    nc.gpsimd.tensor_scalar(p_w[:, u % 2, r, 0:w], p_w[:, u % 2, r, 0:w], w_col(5, u)[:, r:r + 1],
                                            0.5, ALU.mult, ALU.mult).then_inc(s_wp, 1)

            def gate_w(u):
                n, g = u // GROUPS, u % GROUPS
                if u == 0:
                    pool.wait_ge(s_ge, N_WIN_JOB)
                pool.wait_ge(s_wo, u + 1)
                y = Y[:, 2 * g:2 * g + 2, n * P:(n + 1) * P]
                nc.gpsimd.tensor_tensor(y, y, o_w[:, u % 2, :, :], ALU.mult).then_inc(s_wy, 1)

            for m in range(NM - 2):
                split_w(m)
            for s in range(W_UNITS + 2):
                if s < W_UNITS:
                    probs_w(s)
                if s >= 2:
                    gate_w(s - 2)
                if s == 4:
                    split_w(NM - 2)
                if s == 8:
                    split_w(NM - 1)

            def split_piece(h, i):
                hp = h % 2
                if i in (0, 3):
                    raw, hi = (q_raw, q_hi) if i == 0 else (k_raw, k_hi)
                    if i == 0:
                        pool.wait_ge(s_qki, 64 * (h + 1))
                        if h >= 2:
                            pool.wait_ge(s_bs, NT * (h - 1))
                    nc.gpsimd.tensor_scalar(hi[:, hp, :], raw[:, :], 1.0, 1.0, ALU.mult,
                                            ALU.mult).then_inc(s_sph, 1)
                elif i < 6:
                    raw, hi, lo = (q_raw, q_hi, q_lo) if i < 3 else (k_raw, k_hi, k_lo)
                    if i in (1, 4):
                        pool.wait_ge(s_sph, 2 * (h - 1) + 1 + (i == 4))
                    c = slice((i - 1) % 3 * HALF, ((i - 1) % 3 + 1) * HALF)
                    last = nc.gpsimd.tensor_tensor(lo[:, hp, c], raw[:, c], f(hi[:, hp, c]), ALU.subtract)
                    if i in (2, 5):
                        last.then_inc(s_sp, 1)
                elif i == 7:
                    if h >= 2:
                        pool.wait_ge(s_bpv, 2 * (h - 1))
                    raw = v_raw[:, :, h * HD:(h + 1) * HD]
                    split(raw, vB[:, hp, :, 0:HD], vB[:, hp, :, HD:P], s_sph2, h + 1, s_sp2)

            def probs_b(U):
                pool.wait_ge(s_br, U + 1)
                nc.gpsimd.tensor_scalar(p_b[:, U % 4, :], p_b[:, U % 4, :], r_b[:, U % 4:U % 4 + 1], 0.5,
                                        ALU.mult, ALU.mult).then_inc(s_bp, 1)

            def gate_b(j, c):
                pool.wait_ge(s_bo, 4 * j + c + 3)
                if j == 0 and c == 0:
                    pool.wait_ge(s_ge, 2 * NM)
                y = Y[:, 4 + j, c * HALF:(c + 1) * HALF]
                nc.gpsimd.tensor_tensor(y, y, o_b[:, c, :], ALU.mult).then_inc(s_by, 1)

            pool.wait_ge(s_vr, 16)
            split(v_raw[:, :, 0:HD], vB[:, 0, :, 0:HD], vB[:, 0, :, HD:P], s_sph2, 1, s_sp2)
            for U in range(B_UNITS + 8):
                if U < B_UNITS:
                    probs_b(U)
                if U // NT + 1 < HEADS:
                    split_piece(U // NT + 1, U % NT)
                G = (U - 10) // 4
                if U >= 10 and (U - 10) % 4 == 0 and G % 4 >= 2:
                    gate_b(G // 4, G % 2)

            pool.wait_ge(s_bpv, B_GROUPS)
            for k in range(KT):
                pool.wait_ge(s_woi[k % 4], 16 * (k // 4 + 1))
                nc.gpsimd.tensor_scalar(wo_hi[:, k, :], wo_raw[:, k % 4, :], 1.0, 1.0, ALU.mult, ALU.mult) \
                    .then_inc(s_woh, 1)

        @block.scalar
        def _(act):
            def h_hi(t):
                for a in range(2):
                    act.wait_ge(s_xT, 2 * t + a + 1)
                    nc.scalar.activation(hT_hi[:, 4 * a:4 * a + 4, t * P:(t + 1) * P],
                                         ps[:, a, :].rearrange("p (k c) -> p k c", c=P),
                                         ACT.Copy).then_inc(s_hhi, 1)

            for t in range(NT):
                act.wait_ge(s_x[t % 2], 16 * (t // 2 + 1))
                if t >= 2:
                    act.wait_ge(s_xT, 2 * (t - 1))
                nc.scalar.activation(x_n[:, t % 2, :], x_in[:, t % 2, :], ACT.Square,
                                     accum_out=ssq[:, t:t + 1]).then_inc(s_ssq, 1)
                act.wait_ge(s_var, t + 1)
                nc.scalar.activation(rms[:, t:t + 1], var[:, t:t + 1], ACT.Sqrt).then_inc(s_rms, 1)
                if t >= 1:
                    h_hi(t - 1)
            h_hi(NT - 1)

            def lat_hi(t):
                act.wait_ge(s_lT, t + 1)
                nc.scalar.activation(latT_hi[:, 0:4, t * P:(t + 1) * P],
                                     ps[:, 0, :].rearrange("p (k c) -> p k c", c=P), ACT.Copy)
                nc.scalar.activation(latT_hi[:, 4, t * P:(t + 1) * P], ps[:, 1, 0:P],
                                     ACT.Copy).then_inc(s_lhi, 1)

            for t in range(NT):
                a, b = nat_banks(t)
                act.wait_ge(s_pA, t + 1)
                nc.scalar.activation(vA[:, t, :, 0:HD], ps[:, a, 0:P].rearrange("p (g c) -> p g c", c=HD),
                                     ACT.Copy)
                if t >= 2:
                    act.wait_ge(s_lT, t - 1)
                nc.scalar.activation(lat[:, t % 2, QL:QL + KVL], ps[:, a, P:P + KVL], ACT.Square,
                                     accum_out=lss[:, 1:2])
                nc.scalar.activation(kr_n[:, t, :], ps[:, a, P + KVL:NA], ACT.Copy).then_inc(s_va, 1)
                act.wait_ge(s_pB, t + 1)
                nc.scalar.activation(lat[:, t % 2, 0:QL], ps[:, b, 0:QL], ACT.Square,
                                     accum_out=lss[:, 0:1]).then_inc(s_lss, 1)
                if t >= 2:
                    lat_hi(t - 2)
                act.wait_ge(s_lvar, t + 1)
                nc.scalar.activation(lrms, lvar, ACT.Sqrt).then_inc(s_lrms, 1)
            lat_hi(NT - 2)
            lat_hi(NT - 1)

            for j, (kind, t, h) in enumerate(UP):
                if kind in BY_DVE:
                    continue
                act.wait_ge(s_up, j + 1)
                if j >= 4:
                    act.wait_ge(s_st[j % 4], 16 * (j // 4))
                n = ROPE if kind == "kr" else P
                if kind == "q":
                    nc.scalar.activation(stage[:, j % 4, :], ps[:, UP_BANK[j % 4], :], ACT.Copy,
                                         scale=B_SCALE).then_inc(s_upa, 1)
                else:
                    nc.scalar.activation(stage[0:n, j % 4, :], ps[0:n, UP_BANK[j % 4], :],
                                         ACT.Copy).then_inc(s_upa, 1)

            def evac_g(g):
                m, cols, bank = g // 2, slice(g % 2 * HALF, (g % 2 + 1) * HALF), g_bank(g)
                act.wait_ge(s_g, g + 1)
                if m == 0:
                    wait_all_stored(act)
                    for q in range(GROUPS):
                        for half in (0, HD):
                            last = nc.scalar.activation(k_hi2[half:half + HD, q, cols],
                                                        ps[HD * q:HD * (q + 1), bank, :], ACT.Copy)
                elif m < 5:
                    for q in range(2):
                        h = 2 * (m - 1) + q
                        last = nc.scalar.activation(q_st[0:HD, h, cols], ps[HD * q:HD * (q + 1), bank, :],
                                                    ACT.Copy, scale=-A_SCALE / SLOPE[h])
                else:
                    last = nc.scalar.activation(Y[:, m - 5, cols], ps[:, bank, :], ACT.Tanh, scale=0.5)
                last.then_inc(s_ga, 1)

            def exp_w(u, r):
                w = len(w_keys(u)) * P
                act.wait_ge(s_wm, REP * u + r + 1)
                p = p_w[:, u % 2, r, 0:w]
                nc.scalar.activation(p, p, ACT.Exp, bias=w_col(0, u)[:, r:r + 1], scale=-1.0,
                                     accum_out=w_col(3, u)[:, r:r + 1])

            def exp_sink_w(u):
                act.wait_ge(s_wnm, u + 1)
                nc.scalar.activation(w_col(4, u), w_col(2, u), ACT.Exp).then_inc(s_we, 1)

            def pT_w_hi(c):
                act.wait_ge(s_wT, c + 1)
                if c >= 2:
                    act.wait_ge(s_wpv, c - 1)
                nc.scalar.activation(pT_wh[:, c % 2, :], ps[:, 4 + c % 2, :], ACT.Copy).then_inc(s_wTh, 1)

            def o_w_lo(u):
                act.wait_ge(s_wpv, W_FIRST[u + 1])
                if u >= 1:
                    act.wait_ge(s_wo, u)
                nc.scalar.activation(ol_w[:, :], ps[HD:P, 7, :], ACT.Copy).then_inc(s_wol, 1)

            for g in range(N_WIN_JOB):
                evac_g(g)
            def head0_hi():
                act.wait_ge(s_qki, 64)
                act.wait_ge(s_krl, 16)
                act.wait_ge(s_ws, REP * W_UNITS)
                nc.scalar.activation(k_hi[:, 0, :], k_raw[:, :], ACT.Copy).then_inc(s_h0, 1)
                nc.scalar.activation(q_hi[:, 0, :], q_raw[:, :], ACT.Copy).then_inc(s_h0, 1)

            for s in range(W_UNITS + 1):
                keys = range(W_FIRST[s - 1], W_FIRST[s]) if s >= 1 else []
                live = s < W_UNITS
                if s >= 2:
                    if s % 2 == 0:
                        evac_g(N_WIN_JOB + s // 2 - 1)
                    o_w_lo(s - 2)
                if live:
                    exp_w(s, 0)
                else:
                    head0_hi()
                for i, c in enumerate(keys[:2]):
                    pT_w_hi(c)
                    if live:
                        exp_w(s, 1 + i)
                if live:
                    for r in range(1 + len(keys[:2]), REP):
                        exp_w(s, r)
                    exp_sink_w(s)
                for c in keys[2:]:
                    pT_w_hi(c)
            o_w_lo(W_UNITS - 1)

            def exp_b(U):
                act.wait_ge(s_bm, U + 1)
                if U >= 4:
                    act.wait_ge(s_bT, 2 * (U - 3))
                b = 2 * (U % 2)
                nc.scalar.activation(p_b[:, U % 4, :], ps[:, b:b + 2, :].rearrange("p b c -> p (b c)"), ACT.Exp,
                                     bias=nm_b[:, U % 4:U % 4 + 1],
                                     accum_out=sum_b[:, U % 4:U % 4 + 1]).then_inc(s_be, 1)

            def pT_b_hi(U, a):
                act.wait_ge(s_bT, 2 * U + a + 1)
                G = U // 4
                if U % 4 == 0 and a == 0 and G >= 2:
                    act.wait_ge(s_bpv, G - 1)
                nc.scalar.activation(pT_hi[:, G % 2, 4 * a:4 * a + 4, U % 4 * P:(U % 4 + 1) * P],
                                     ps[:, 4 + a, :].rearrange("p (k c) -> p k c", c=P),
                                     ACT.Copy).then_inc(s_bTh, 1)

            def o_b_lo(G):
                act.wait_ge(s_bpv, G + 1)
                if G >= 1:
                    act.wait_ge(s_bo, G)
                nc.scalar.activation(ol_b[:, :], ps[HD:P, 6 + G % 2, :], ACT.Copy).then_inc(s_bol, 1)

            for U in range(B_UNITS + 7):
                if 2 <= U < B_UNITS + 2:
                    pT_b_hi(U - 2, 0)
                    pT_b_hi(U - 2, 1)
                if U < B_UNITS:
                    exp_b(U)
                if U >= 9 and (U - 9) % 4 == 0:
                    o_b_lo((U - 9) // 4)

            for k in range(KT):
                if k == 0:
                    act.wait_ge(s_sp, 2 * (HEADS - 1))
                    act.wait_ge(s_sp2, HEADS)
                    act.wait_ge(s_bs, B_UNITS)
                    act.wait_ge(s_by, B_GROUPS // 2)
                nc.scalar.activation(y_hi[:, k, :], Y[:, k, :], ACT.Copy).then_inc(s_yh, 1)
            for t in range(NT):
                act.wait_ge(s_oadd, t + 1)
                nc.scalar.activation(x_r[:, t % 2, :], o_n[:, t % 2, :], ACT.Square,
                                     accum_out=ssq[:, t:t + 1]).then_inc(s_oss, 1)
                act.wait_ge(s_ovar, t + 1)
                nc.scalar.activation(rms[:, t:t + 1], var[:, t:t + 1], ACT.Sqrt).then_inc(s_orms, 1)

        @block.vector
        def _(dve):
            chain = [0]

            def link(ins):
                chain[0] += 1
                ins.then_inc(s_chain, 1)
                dve.wait_ge(s_chain, chain[0])

            def h_lo(t):
                for a in range(2):
                    dve.wait_ge(s_hhi, 2 * t + a + 1)
                    nc.vector.tensor_tensor(hT_lo[:, 4 * a:4 * a + 4, t * P:(t + 1) * P],
                                            ps[:, a, :].rearrange("p (k c) -> p k c", c=P),
                                            f(hT_hi[:, 4 * a:4 * a + 4, t * P:(t + 1) * P]),
                                            ALU.subtract).then_inc(s_hT, 1)

            dve.wait_ge(s_gmix, 16)
            for t in range(NT):
                dve.wait_ge(s_ssq, t + 1)
                nc.vector.tensor_scalar(var[:, t:t + 1], ssq[:, t:t + 1], 1.0 / D, EPS, ALU.mult,
                                        ALU.add).then_inc(s_var, 1)
                dve.wait_ge(s_rms, t + 1)
                link(nc.vector.reciprocal(rstd[:, t:t + 1], rms[:, t:t + 1]))
                nc.vector.scalar_tensor_tensor(out=x_n[:, t % 2, :], in0=x_in[:, t % 2, :],
                                               scalar=rstd[:, t:t + 1], in1=g_mix[:, :], op0=ALU.mult,
                                               op1=ALU.mult).then_inc(s_xn, 1)
                if t >= 1:
                    h_lo(t - 1)
            h_lo(NT - 1)

            def lat_lo(t):
                dve.wait_ge(s_lhi, t + 1)
                cols = slice(t * P, (t + 1) * P)
                nc.vector.tensor_tensor(latT_lo[:, 0:4, cols], ps[:, 0, :].rearrange("p (k c) -> p k c", c=P),
                                        f(latT_hi[:, 0:4, cols]), ALU.subtract)
                nc.vector.tensor_tensor(latT_lo[:, 4, cols], ps[:, 1, 0:P], f(latT_hi[:, 4, cols]),
                                        ALU.subtract).then_inc(s_latT, 1)

            dve.wait_ge(s_glat, 32)
            for t in range(NT):
                a, b = nat_banks(t)
                dve.wait_ge(s_va, t + 1)
                nc.vector.tensor_tensor(vA[:, t, :, HD:P], ps[:, a, 0:P].rearrange("p (g c) -> p g c", c=HD),
                                        f(vA[:, t, :, 0:HD]), ALU.subtract)
                dve.wait_ge(s_lss, t + 1)
                nc.vector.tensor_scalar(lvar[:, 0:1], lss[:, 0:1], 1.0 / QL, EPS, ALU.mult, ALU.add)
                nc.vector.tensor_scalar(lvar[:, 1:2], lss[:, 1:2], 1.0 / KVL, EPS, ALU.mult,
                                        ALU.add).then_inc(s_lvar, 1)
                if t >= 2:
                    lat_lo(t - 2)
                dve.wait_ge(s_lrms, t + 1)
                link(nc.vector.reciprocal(lrstd, lrms))
                nc.vector.scalar_tensor_tensor(out=lat[:, t % 2, 0:QL], in0=ps[:, b, 0:QL],
                                               scalar=lrstd[:, 0:1], in1=g_lat[:, 0:QL], op0=ALU.mult,
                                               op1=ALU.mult)
                nc.vector.scalar_tensor_tensor(out=lat[:, t % 2, QL:QL + KVL], in0=ps[:, a, P:P + KVL],
                                               scalar=lrstd[:, 1:2], in1=g_lat[:, QL:QL + KVL],
                                               op0=ALU.mult, op1=ALU.mult).then_inc(s_lat, 1)
            lat_lo(NT - 2)
            lat_lo(NT - 1)
            dve.wait_ge(s_rnat, 16)
            x1, x2, cos, sin = kr_n[:, :, 0:HR], kr_n[:, :, HR:ROPE], r_nat[:, 0, :, :], r_nat[:, 1, :, :]
            for i, (a, b) in enumerate(((x1, cos), (x2, sin), (x1, sin), (x2, cos))):
                last = nc.vector.tensor_tensor(kr_t[:, i, :, :], a, b, ALU.mult)
            link(last)
            nc.vector.tensor_tensor(kr_r[:, :, 0:HR], kr_t[:, 0, :, :], kr_t[:, 1, :, :], ALU.subtract)
            nc.vector.tensor_tensor(kr_r[:, :, HR:ROPE], kr_t[:, 2, :, :], kr_t[:, 3, :, :],
                                    ALU.add).then_inc(s_krr, 1)

            dve.wait_ge(s_rq, 16)
            for j, (kind, t, h) in enumerate(UP):
                if kind == "r" and t == 1:
                    x1, x2 = ps[:, UP_BANK[(j - 1) % 4], :], ps[:, UP_BANK[j % 4], :]
                    cos, sin = (r_q[:, i, h * HALF:(h + 1) * HALF] for i in range(2))
                    dve.wait_ge(s_up, j + 1)
                    if h == 1:
                        dve.wait_ge(s_upd, 2)
                    for i in (j - 1, j):
                        dve.wait_ge(s_st[i % 4], 16 * (i // 4))
                    for i, (a, b) in enumerate(((x1, cos), (x2, sin), (x1, sin), (x2, cos))):
                        last = nc.vector.tensor_tensor(r_tmp[:, i, :], a, b, ALU.mult)
                    link(last)
                    nc.vector.tensor_tensor(stage[:, (j - 1) % 4, :], r_tmp[:, 0, :], r_tmp[:, 1, :],
                                            ALU.subtract)
                    nc.vector.tensor_tensor(stage[:, j % 4, :], r_tmp[:, 2, :], r_tmp[:, 3, :],
                                            ALU.add).then_inc(s_upd, 2)
                if kind == "v":
                    dve.wait_ge(s_up, j + 1)
                    dve.wait_ge(s_st[j % 4], 16 * (j // 4))
                    nc.vector.tensor_copy(stage[:, j % 4, :], ps[:, UP_BANK[j % 4], :]).then_inc(s_upd, 1)

            def evac_g(g):
                m, cols, bank = g // 2, slice(g % 2 * HALF, (g % 2 + 1) * HALF), g_bank(g)
                dve.wait_ge(s_ga, g + 1)
                if m == 0:
                    for q in range(GROUPS):
                        for half in (0, HD):
                            last = nc.vector.tensor_tensor(k_lo2[half:half + HD, q, cols],
                                                           ps[HD * q:HD * (q + 1), bank, :],
                                                           f(k_hi2[half:half + HD, q, cols]), ALU.subtract)
                elif m < 5:
                    for q in range(2):
                        h = 2 * (m - 1) + q
                        last = nc.vector.scalar_tensor_tensor(
                            out=q_st[HD:P, h, cols], in0=ps[HD * q:HD * (q + 1), bank, :],
                            scalar=-A_SCALE / SLOPE[h], in1=f(q_st[0:HD, h, cols]), op0=ALU.mult,
                            op1=ALU.subtract)
                else:
                    last = nc.vector.scalar_tensor_tensor(out=Y[:, m - 5, cols], in0=Y[:, m - 5, cols],
                                                          scalar=1.0, in1=ps[:, bank, :], op0=ALU.add,
                                                          op1=ALU.mult)
                last.then_inc(s_ge, 1)

            def max_w(u, r):
                n, g, keys = u // GROUPS, u % GROUPS, w_keys(u)
                c0, w = (keys[0] - (n - 1)) * P, len(keys) * P
                h = REP * g + r
                if u >= 2 and r == 0:
                    dve.wait_ge(s_wT, W_FIRST[u - 1])
                dve.wait_ge(s_ws, REP * u + r + 1)
                nc.vector.tensor_tensor_reduce(out=p_w[:, u % 2, r, 0:w], in0=distb[:, c0:c0 + w],
                                               in1=ps[:, r, 0:w], scale=SLOPE[h],
                                               scalar=nsink[:, h:h + 1], op0=ALU.add, op1=ALU.min,
                                               accum_out=w_col(0, u)[:, r:r + 1]).then_inc(s_wm, 1)

            def sink_w(u):
                g = u % GROUPS
                dve.wait_ge(s_wm, REP * (u + 1))
                nc.vector.tensor_tensor(w_col(2, u), w_col(0, u), nsink[:, REP * g:REP * (g + 1)],
                                        ALU.subtract).then_inc(s_wnm, 1)

            def recip_w(u):
                dve.wait_ge(s_we, u + 1)
                link(nc.vector.tensor_tensor(w_col(4, u), w_col(3, u), w_col(4, u), ALU.add))
                nc.vector.reciprocal(w_col(5, u), w_col(4, u)).then_inc(s_wrd, 1)
                dve.wait_ge(s_wrd, u + 1)
                w = len(w_keys(u)) * P
                for r in range(POOL_R, REP):
                    last = nc.vector.tensor_scalar(p_w[:, u % 2, r, 0:w], p_w[:, u % 2, r, 0:w],
                                                   w_col(5, u)[:, r:r + 1], 0.5, ALU.mult, ALU.mult)
                last.then_inc(s_wpd, 1)

            def pT_w_lo(c):
                dve.wait_ge(s_wTh, c + 1)
                nc.vector.tensor_tensor(pT_wl[:, c % 2, :], ps[:, 4 + c % 2, :], f(pT_wh[:, c % 2, :]),
                                        ALU.subtract).then_inc(s_wTl, 1)

            def o_w_sum(u):
                dve.wait_ge(s_wol, u + 1)
                if u >= 2:
                    dve.wait_ge(s_wy, u - 1)
                for q in range(2):
                    src = ps[0:HD, 7, :].rearrange("p (a b c) -> p a b c", b=2, c=P)[:, :, q, :]
                    low = ol_w[:, :].rearrange("p (a b c) -> p a b c", b=2, c=P)[:, :, q, :]
                    last = nc.vector.tensor_tensor(o_w[HD * q:HD * (q + 1), u % 2, :, :], src, low, ALU.add)
                last.then_inc(s_wo, 1)

            for g in range(N_WIN_JOB):
                evac_g(g)
            dve.wait_ge(s_dist, 16)
            dve.wait_ge(s_sink, 16)
            link(nc.vector.tensor_scalar(nsink[:, :], sinkb[:, :], -1.0, None, ALU.mult))
            def head0_lo():
                for i, (raw, hi, lo) in enumerate(((k_raw, k_hi, k_lo), (q_raw, q_hi, q_lo))):
                    dve.wait_ge(s_h0, i + 1)
                    last = nc.vector.tensor_tensor(lo[:, 0, :], raw[:, :], f(hi[:, 0, :]), ALU.subtract)
                last.then_inc(s_h0l, 1)

            for s in range(W_UNITS + 1):
                keys = range(W_FIRST[s - 1], W_FIRST[s]) if s >= 1 else []
                live = s < W_UNITS
                if live:
                    max_w(s, 0)
                if s >= 2:
                    if s % 2 == 0:
                        evac_g(N_WIN_JOB + s // 2 - 1)
                    o_w_sum(s - 2)
                if live:
                    max_w(s, 1)
                    max_w(s, 2)
                else:
                    head0_lo()
                if s >= 1:
                    pT_w_lo(keys[0])
                if live:
                    max_w(s, 3)
                    sink_w(s)
                if s >= 1:
                    pT_w_lo(keys[1])
                if live:
                    recip_w(s)
                for c in keys[2:]:
                    pT_w_lo(c)
            o_w_sum(W_UNITS - 1)

            def max_b(U):
                dve.wait_ge(s_bs, U + 1)
                b = 2 * (U % 2)
                nc.vector.tensor_reduce(nm_b[:, U % 4:U % 4 + 1], ps[:, b:b + 2, :].rearrange("p b c -> p (b c)"),
                                        AX.X, ALU.max, negate=True).then_inc(s_bm, 1)

            def recip_b(U):
                dve.wait_ge(s_be, U + 1)
                nc.vector.reciprocal(r_b[:, U % 4:U % 4 + 1], sum_b[:, U % 4:U % 4 + 1]).then_inc(s_br, 1)

            def pT_b_lo(U, a):
                dve.wait_ge(s_bTh, 2 * U + a + 1)
                at_ = (slice(None), U // 4 % 2, slice(4 * a, 4 * a + 4), slice(U % 4 * P, (U % 4 + 1) * P))
                nc.vector.tensor_tensor(pT_lo[at_], ps[:, 4 + a, :].rearrange("p (k c) -> p k c", c=P),
                                        f(pT_hi[at_]), ALU.subtract).then_inc(s_bTl, 1)

            def o_b_sum(G):
                q = HD * (G // 2 % 2)
                dve.wait_ge(s_bol, G + 1)
                if G % 4 < 2 and G >= 4:
                    dve.wait_ge(s_by, 2 * (G // 4 - 1) + G % 2 + 1)
                nc.vector.tensor_tensor(o_b[q:q + HD, G % 2, :], ps[0:HD, 6 + G % 2, :], ol_b[:, :],
                                        ALU.add).then_inc(s_bo, 1)

            for U in range(B_UNITS + 7):
                if 1 <= U <= B_UNITS:
                    recip_b(U - 1)
                if U < B_UNITS:
                    max_b(U)
                if 2 <= U < B_UNITS + 2:
                    pT_b_lo(U - 2, 0)
                    pT_b_lo(U - 2, 1)
                if U >= 9 and (U - 9) % 4 == 0:
                    o_b_sum((U - 9) // 4)

            for k in range(KT):
                dve.wait_ge(s_yh, k + 1)
                nc.vector.tensor_tensor(y_lo[:, k, :], Y[:, k, :], f(y_hi[:, k, :]), ALU.subtract).then_inc(s_yl, 1)
                dve.wait_ge(s_woh, k + 1)
                nc.vector.tensor_tensor(wo_lo[:, k, :], wo_raw[:, k % 4, :], f(wo_hi[:, k, :]),
                                        ALU.subtract).then_inc(s_wol2, 1)
            dve.wait_ge(s_gfin, 16)
            for t in range(NT):
                b = 2 * (t % 4)
                dve.wait_ge(s_op, t + 1)
                dve.wait_ge(s_xr[t % 2], 16 * (t // 2 + 1))
                if t >= 2:
                    dve.wait_ge(s_out[t % 2], 16 * (t // 2))
                nc.vector.tensor_tensor(o_n[:, t % 2, :], ps[:, b:b + 2, :].rearrange("p b c -> p (b c)"),
                                        x_r[:, t % 2, :], ALU.add).then_inc(s_oadd, 1)
                dve.wait_ge(s_oss, t + 1)
                nc.vector.tensor_scalar(var[:, t:t + 1], ssq[:, t:t + 1], 1.0 / D, EPS, ALU.mult,
                                        ALU.add).then_inc(s_ovar, 1)
                dve.wait_ge(s_orms, t + 1)
                link(nc.vector.reciprocal(rstd[:, t:t + 1], rms[:, t:t + 1]))
                nc.vector.scalar_tensor_tensor(out=o_n[:, t % 2, :], in0=o_n[:, t % 2, :],
                                               scalar=rstd[:, t:t + 1], in1=g_fin[:, :], op0=ALU.mult,
                                               op1=ALU.mult).then_inc(s_on, 1)

        @block.tensor
        def _(pe):
            def three(o, a_hi, a_lo, b_hi, b_lo, first, last):
                nc.tensor.matmul(o, a_hi, b_hi, start=first, stop=False)
                nc.tensor.matmul(o, a_hi, b_lo, start=False, stop=False)
                return nc.tensor.matmul(o, a_lo, b_hi, start=False, stop=last)

            def turn_x(t):
                pe.wait_ge(s_xn, t + 1)
                for a in range(2):
                    if t >= 1:
                        pe.wait_ge(s_hT, 2 * t - 1 + a)
                    for k in range(4):
                        c = 4 * a + k
                        last = nc.tensor.transpose(ps[:, a, k * P:(k + 1) * P], x_n[:, t % 2, c * P:(c + 1) * P],
                                                   ident[:, :])
                    last.then_inc(s_xT, 1)

            def natural(t, c, ks):
                w0, w1 = ((0, NA), (NA, NW))[c]
                toks = slice(t * P, (t + 1) * P)
                for k in ks:
                    last = three(ps[:, nat_banks(t)[c], 0:w1 - w0], hT_hi[:, k, toks], hT_lo[:, k, toks],
                                 wn_hi[:, k, w0:w1], wn_lo[:, k, w0:w1], k == 0, k == KT - 1)
                if ks[-1] == KT - 1:
                    last.then_inc((s_pA, s_pB)[c], 1)

            def turn_lat(t):
                pe.wait_ge(s_lat, t + 1)
                if t == 0:
                    pe.wait_ge(s_hT, 2 * NT)
                else:
                    pe.wait_ge(s_latT, t)
                for k in range(LT):
                    last = nc.tensor.transpose(ps[:, k // 4, k % 4 * P:(k % 4 + 1) * P],
                                               lat[:, t % 2, k * P:(k + 1) * P], ident[:, :])
                last.then_inc(s_lT, 1)

            pe.wait_ge(s_id, 2)
            for t in range(3):
                turn_x(t)
            pe.wait_ge(s_hT, 2 * 3)
            for k in range(KT - 2):
                pe.wait_ge(s_wnr, k + 1)
                for t in range(3):
                    for c in range(2):
                        natural(t, c, range(k, k + 1))
                if k < NT - 3:
                    turn_x(3 + k)
            pe.wait_ge(s_wnr, KT)
            for t in range(3):
                for c in range(2):
                    natural(t, c, range(KT - 2, KT))
            for t in range(3, NT):
                pe.wait_ge(s_hT, 2 * (t + 1))
                pe.wait_ge(s_lat, t - 2)
                natural(t, 0, range(KT))
                if t == 3:
                    turn_lat(0)
                natural(t, 1, range(KT))
                turn_lat(t - 2)

            for j, (kind, t, h) in enumerate(UP):
                o = ps[:, UP_BANK[j % 4], :]
                cols = slice(h * HALF, (h + 1) * HALF)
                if j in (2, 3):
                    turn_lat(j + 4)
                if j == 0:
                    pe.wait_ge(s_latT, 4)
                    pe.wait_ge(s_uq, 1)
                elif j == 2:
                    pe.wait_ge(s_lat, 7)
                if (kind, t, h) == ("q", 0, 1):
                    pe.wait_ge(s_latT, NT)
                if kind == "kr" and h == 0:
                    pe.wait_ge(s_krr, 1)
                if kind == "k" and t == 0 and h == 0:
                    pe.wait_ge(s_ukv, 1)
                if j >= 4:
                    wait_up_copied(pe, j - 4)
                if kind in ("r", "q"):
                    c = 4 + t if kind == "r" else t
                    for k in range(QLT):
                        last = three(o, uq_hi[:, k, c, :], uq_lo[:, k, c, :], latT_hi[:, k, cols],
                                     latT_lo[:, k, cols], k == 0, k == QLT - 1)
                elif kind == "kr":
                    for i in range(4):
                        last = nc.tensor.transpose(o[0:ROPE, i * P:(i + 1) * P], kr_r[:, 4 * h + i, :], ident[:, :])
                elif kind == "k":
                    for k in range(KVLT):
                        wh, wl = (a[:, k, 2 * t:2 * t + 2, :].rearrange("p a c -> p (a c)") for a in (uk_hi, uk_lo))
                        last = three(o, wh, wl, latT_hi[:, QLT + k, cols], latT_lo[:, QLT + k, cols],
                                     k == 0, k == KVLT - 1)
                else:
                    toks = slice(t * P, (t + 1) * P)
                    for k in range(KVLT):
                        wh, wl = (a[:, k, :, :].rearrange("p a c -> p (a c)") for a in (uv_hi, uv_lo))
                        last = three(o, latT_hi[:, QLT + k, toks], latT_lo[:, QLT + k, toks], wh, wl,
                                     k == 0, k == KVLT - 1)
                last.then_inc(s_up, 1)

            def gated(g, ks):
                m, cols = g // 2, slice(g % 2 * HALF, (g % 2 + 1) * HALF)
                if ks[0] == 0:
                    pe.wait_ge(s_wr, m + 1)
                    if g < 2:
                        wait_up_copied(pe, len(UP) - 2 + g)
                    else:
                        pe.wait_ge(s_ge, g if g > N_WIN_JOB else g - 1)
                for k in ks:
                    last = three(ps[:, g_bank(g), :], w_hi[:, m % 2, k, :], w_lo[:, m % 2, k, :],
                                 hT_hi[:, k, cols], hT_lo[:, k, cols], k == 0, k == KT - 1)
                if ks[-1] == KT - 1:
                    last.then_inc(s_g, 1)

            def scores_w(u):
                n, g, keys = u // GROUPS, u % GROUPS, w_keys(u)
                k0, w = keys[0] * P, len(keys) * P
                for r in range(REP):
                    if u >= 1:
                        pe.wait_ge(s_wm, REP * (u - 1) + r + 1)
                    q = q_st[:, REP * g + r, n * P:(n + 1) * P]
                    nc.tensor.matmul(ps[:, r, 0:w], q, k_hi2[:, g, k0:k0 + w], start=True, stop=False)
                    nc.tensor.matmul(ps[:, r, 0:w], q, k_lo2[:, g, k0:k0 + w], start=False,
                                     stop=True).then_inc(s_ws, 1)

            def turn_w(u, i):
                c = W_FIRST[u] + i
                if i == 0:
                    pe.wait_ge(s_wp, POOL_R * (u + 1))
                    pe.wait_ge(s_wpd, u + 1)
                if c >= 2:
                    pe.wait_ge(s_wTl, c - 1)
                elif c == 0:
                    pe.wait_ge(s_lat, NT)
                for r in range(REP):
                    last = nc.tensor.transpose(ps[:, 4 + c % 2, r * P:(r + 1) * P],
                                               p_w[:, u % 2, r, i * P:(i + 1) * P], ident[:, :])
                last.then_inc(s_wT, 1)

            def pv_w(u, i):
                c, keys = W_FIRST[u] + i, w_keys(u)
                if i == 0:
                    pe.wait_ge(s_wo, u) if u else pe.wait_ge(s_ge, N_WIN_JOB)
                pe.wait_ge(s_wTl, c + 1)
                v = vA[:, keys[i], u % GROUPS, :]
                nc.tensor.matmul(ps[:, 7, :], v, pT_wh[:, c % 2, :], start=(i == 0), stop=False)
                nc.tensor.matmul(ps[:, 7, :], v, pT_wl[:, c % 2, :], start=False,
                                 stop=(i == len(keys) - 1)).then_inc(s_wpv, 1)

            def scores_b(U):
                h, t, hp = U // NT, U % NT, U // NT % 2
                if t == 0:
                    if h == 0:
                        pe.wait_ge(s_h0l, 1)
                    else:
                        pe.wait_ge(s_sp, 2 * h)
                if U >= 2:
                    pe.wait_ge(s_be, U - 1)
                q = slice(t * P, (t + 1) * P)
                for c in range(2):
                    k = slice(c * HALF, (c + 1) * HALF)
                    last = three(ps[:, 2 * (U % 2) + c, :], q_hi[:, hp, q], q_lo[:, hp, q], k_hi[:, hp, k],
                                 k_lo[:, hp, k], True, True)
                last.then_inc(s_bs, 1)

            for g in range(N_WIN_JOB):
                gated(g, range(KT))
            for s in range(W_UNITS + 1):
                g, k0 = N_WIN_JOB + s // 2, 4 * (s % 2)
                n = len(w_keys(s - 1)) if s >= 1 else 0
                if s < W_UNITS:
                    scores_w(s)
                if n:
                    turn_w(s - 1, 0)
                    turn_w(s - 1, 1)
                if s < W_UNITS:
                    gated(g, range(k0, k0 + 2))
                else:
                    pe.wait_ge(s_wm, REP * W_UNITS)
                    scores_b(0)
                    scores_b(1)
                if n:
                    pv_w(s - 1, 0)
                    if n > 2:
                        turn_w(s - 1, 2)
                if s < W_UNITS:
                    gated(g, range(k0 + 2, k0 + 4))
                for i in range(1, n):
                    pv_w(s - 1, i)

            def turn_b(U):
                pe.wait_ge(s_bp, U + 1)
                for a in range(2):
                    if U >= 1:
                        pe.wait_ge(s_bTl, 2 * (U - 1) + a + 1)
                    else:
                        pe.wait_ge(s_wTl, W_FIRST[W_UNITS])
                    for k in range(4):
                        last = nc.tensor.transpose(ps[:, 4 + a, k * P:(k + 1) * P],
                                                   p_b[:, U % 4, (4 * a + k) * P:(4 * a + k + 1) * P], ident[:, :])
                    last.then_inc(s_bT, 1)

            def pv_b(G, part):
                hp = G // 2 % 2
                if part == 0:
                    pe.wait_ge(s_sp2, G // 2 + 1)
                    pe.wait_ge(s_bTl, 8 * (G + 1))
                    if G >= 2:
                        pe.wait_ge(s_bo, G - 1)
                    else:
                        pe.wait_ge(s_wo, W_UNITS)
                        pe.wait_ge(s_ge, 2 * NM)
                for k in (2 * part, 2 * part + 1):
                    o = ps[:, 6 + G % 2, :]
                    nc.tensor.matmul(o, vB[:, hp, k, :], pT_hi[:, G % 2, k, :], start=(k == 0), stop=False)
                    last = nc.tensor.matmul(o, vB[:, hp, k, :], pT_lo[:, G % 2, k, :], start=False,
                                            stop=(k == NT - 1))
                if part == 3:
                    last.then_inc(s_bpv, 1)

            for U in range(B_UNITS + 6):
                if 2 <= U < B_UNITS:
                    scores_b(U)
                if 2 <= U < B_UNITS + 2:
                    turn_b(U - 2)
                if U >= 6:
                    pv_b((U - 6) // 4, (U - 6) % 4)

            for t0 in range(0, NT, 4):
                order = [(k, t) for k in range(KT) for t in range(t0, t0 + 4)] if t0 == 0 else \
                    [(k, t) for t in range(t0, t0 + 4) for k in range(KT)]
                for k, t in order:
                    if t0 == 0 and t == 0:
                        pe.wait_ge(s_yl, k + 1)
                        pe.wait_ge(s_wol2, k + 1)
                        if k == 0:
                            pe.wait_ge(s_be, B_UNITS)
                            pe.wait_ge(s_bTl, 2 * B_UNITS)
                            pe.wait_ge(s_bo, B_GROUPS)
                    if t0 and k == 0:
                        pe.wait_ge(s_oadd, t - 3)
                    for c in range(2):
                        last = three(ps[:, 2 * (t % 4) + c, :], y_hi[:, k, t * P:(t + 1) * P],
                                     y_lo[:, k, t * P:(t + 1) * P], wo_hi[:, k, c * HALF:(c + 1) * HALF],
                                     wo_lo[:, k, c * HALF:(c + 1) * HALF], k == 0, k == KT - 1)
                    if k == KT - 1:
                        last.then_inc(s_op, 1)


def _constants():
    pos = np.arange(SEQ, dtype=np.float32)
    inv = np.float32(10000.0) ** (-np.arange(0, ROPE, 2, dtype=np.float32) / np.float32(ROPE))
    ang = pos[:, None] * inv[None, :]
    cs = np.stack([np.cos(ang), np.sin(ang)]).astype(np.float32)
    nat = cs.reshape(2, NT, P, HR).transpose(2, 0, 1, 3)
    q = np.tile(cs.transpose(0, 2, 1), (1, HEADS, 1)).transpose(1, 0, 2)
    q = q.astype(np.float64) * B_SCALE
    away = np.abs(np.arange(P)[:, None] - np.arange(3 * P)[None, :] + P)
    dist = np.where(away <= P, away.astype(np.float32), np.float32(MASKED))
    return {"rope_nat": nat.astype(np.float32), "rope_q": q.astype(np.float32),
            "dist": dist.astype(np.float32)}


_INS = ["x", "norm_mix", "w_in", "attn_sink", "q_a_norm", "w_uq", "kv_a_norm", "w_ukv", "w_out", "final_norm"]


def kernel(**inputs):
    import concourse.bacc as _bacc
    from concourse.bass_utils import run_bass_kernel_spmd as _run

    nc = _bacc.Bacc("TRN2", target_bir_lowering=False, num_devices=1)
    arrays, args = {}, {}
    for name in _INS:
        a = np.ascontiguousarray(inputs[name])
        if name != "final_norm":
            a = a[0]
        arrays[name] = np.ascontiguousarray(a)
    for name, a in _constants().items():
        arrays[name] = np.ascontiguousarray(a)
    for name, a in arrays.items():
        args[name] = nc.dram_tensor(name, a.shape, mybir.dt.from_np(a.dtype), kind="ExternalInput").ap()
    out = nc.dram_tensor("out", (SEQ, D), F32, kind="ExternalOutput").ap()
    encoder(nc, out=out, **args)
    r = _run(nc, [arrays], core_ids=[0])
    return r.results[0]["out"].reshape(1, SEQ, D)
```

```python
from contextlib import ExitStack

import numpy as np

import concourse.bass as bass
from concourse import mybir

F32 = mybir.dt.float32
F32R = mybir.dt.float32r
ALU = mybir.AluOpType
ACT = mybir.ActivationFunctionType
AX = mybir.AxisListType

P = 128
SEQ = 1024
D = 1024
NT = SEQ // P
KT = D // P
HALF = 512
HEADS = 8
HD = 64
GROUPS = 2
REP = HEADS // GROUPS
ROPE = 32
HR = ROPE // 2
QK = HD + ROPE
QL = 384
KVL = 256
QLT = QL // P
KVLT = KVL // P
LT = QLT + KVLT
A_SCALE = HD ** -0.5
B_SCALE = QK ** -0.5
EPS = 1e-6
MASKED = 1e30

QA, KA, VA, GA, CQ = 0, 512, 640, 768, 1280
CKV = CQ + QL
KR = CKV + KVL
GB = KR + ROPE
NA = P + KVL + ROPE
NW = NA + QL

BASE = 16512
POOL_R = 3
SLOPE = [2.0 ** -(h + 1) for h in range(HEADS)]


def f(ap):
    return ap.bitcast(F32)


def encoder(nc, x, norm_mix, w_in, attn_sink, q_a_norm, w_uq, kv_a_norm, w_ukv, w_out, final_norm,
            rope_nat, rope_q, dist, out):
    q_scr = nc.dram_tensor("q_nope_scratch", [HEADS * HD, SEQ], F32, kind="Internal").ap()
    qr_scr = nc.dram_tensor("q_rope_scratch", [2, P, SEQ], F32, kind="Internal").ap()
    k_scr = nc.dram_tensor("k_nope_scratch", [HEADS * HD, SEQ], F32, kind="Internal").ap()
    kr_scr = nc.dram_tensor("k_rope_scratch", [ROPE, SEQ], F32, kind="Internal").ap()
    v_scr = nc.dram_tensor("v_scratch", [SEQ, HEADS * HD], F32, kind="Internal").ap()

    with ExitStack() as ctx:
        def sem(name):
            return ctx.enter_context(nc.semaphore(name))

        def at(name, kb, shape, dt=F32):
            return nc.alloc_sbuf_tensor_at(name, shape, dt, offset=BASE + int(kb * 1024))

        ident = at("ident", 0, [P, P])
        stat = at("stat", 0.5, [P, 96])
        sinkb = at("sinkb", 0.875, [P, HEADS])
        nsink = at("nsink", 0.90625, [P, HEADS])
        hT_hi = at("hT_hi", 1, [P, KT, SEQ], F32R)
        hT_lo = at("hT_lo", 33, [P, KT, SEQ], F32R)
        wn_hi = at("wn_hi", 65, [P, KT, NW], F32R)
        wn_lo = at("wn_lo", 90, [P, KT, NW], F32R)
        wn_raw = at("wn_raw", 115, [P, 3, NW])
        x_in = at("x_in", 124.5, [P, 2, D])
        x_n = at("x_n", 132.5, [P, 2, D])
        g_mix = at("g_mix", 140.5, [P, D])
        g_lat = at("g_lat", 144.5, [P, QL + KVL])
        lat = at("lat", 147, [P, 2, QL + KVL])
        kr_n = at("kr_n", 152, [P, NT, ROPE])
        kr_r = at("kr_r", 153, [P, NT, ROPE])
        kr_t = at("kr_t", 154, [P, 4, NT, HR])
        r_nat = at("r_nat", 156, [P, 2, NT, HR])
        vA = at("vA", 157, [P, NT, GROUPS, P], F32R)
        latT_hi = at("latT_hi", 165, [P, LT, SEQ], F32R)
        latT_lo = at("latT_lo", 185, [P, LT, SEQ], F32R)
        uq_raw = at("uq_raw", 115, [P, QLT, HEADS, QK])
        uq_hi = at("uq_hi", 124.5, [P, QLT, 6, P], F32R)
        uq_lo = at("uq_lo", 133.5, [P, QLT, 6, P], F32R)
        ukv_raw = at("ukv_raw", 65, [P, KVLT, HEADS, P])
        uk_hi = at("uk_hi", 73, [P, KVLT, HEADS, HD], F32R)
        uk_lo = at("uk_lo", 77, [P, KVLT, HEADS, HD], F32R)
        uv_hi = at("uv_hi", 81, [P, KVLT, HEADS, HD], F32R)
        uv_lo = at("uv_lo", 85, [P, KVLT, HEADS, HD], F32R)
        stage = at("stage", 89, [P, 4, HALF])
        r_tmp = at("r_tmp", 97, [P, 4, HALF])
        r_q = at("r_q", 105, [P, 2, SEQ])
        q_st = at("q_st", 65, [P, HEADS, SEQ], F32R)
        k_hi2 = at("k_hi2", 97, [P, GROUPS, SEQ], F32R)
        k_lo2 = at("k_lo2", 105, [P, GROUPS, SEQ], F32R)
        o_w = at("o_w", 113, [P, 2, 2, P])
        w_raw = at("w_raw", 115, [P, 2, KT, P])
        w_hi = at("w_hi", 124.5, [P, 2, KT, P], F32R)
        w_lo = at("w_lo", 132.5, [P, 2, KT, P], F32R)
        distb = at("distb", 140.5, [P, 3 * P])
        p_w = at("p_w", 142, [P, 2, REP, 3 * P])
        ol_w = at("ol_w", 154, [HD, HALF])
        pT_wh = at("pT_wh", 197, [P, 2, HALF], F32R)
        pT_wl = at("pT_wl", 201, [P, 2, HALF], F32R)
        Y = at("Y", 165, [P, KT, SEQ])
        pT_hi = at("pT_hi", 1, [P, 2, NT, HALF], F32R)
        pT_lo = at("pT_lo", 33, [P, 2, NT, HALF], F32R)
        q_hi = at("q_hi", 65, [QK, 2, SEQ], F32R)
        q_lo = at("q_lo", 73, [QK, 2, SEQ], F32R)
        k_hi = at("k_hi", 81, [QK, 2, SEQ], F32R)
        k_lo = at("k_lo", 89, [QK, 2, SEQ], F32R)
        v_raw = at("v_raw", 97, [P, NT, HEADS * HD])
        ol_b = at("ol_b", 113, [HD, HALF])
        q_raw = at("q_raw", 115, [QK, SEQ])
        k_raw = at("k_raw", 119, [QK, SEQ])
        vB = at("vB", 124.5, [P, 2, NT, P], F32R)
        p_b = at("p_b", 132.5, [P, 4, SEQ])
        wo_raw = at("wo_raw", 148.5, [P, 4, D])
        o_b = at("o_b", 197, [P, 2, HALF])
        OUT_KB = {"y_hi": (65, 73, 81, 5, 69, 37, 21, 53), "y_lo": (97, 101, 124.5, 9, 77, 41, 25, 57),
                  "wo_hi": (115, 105, 89, 13, 85, 45, 29, 61), "wo_lo": (119, 109, 1, 33, 93, 17, 49, 128.5)}
        y_hi, y_lo, wo_hi, wo_lo = ([at(f"{n}{k}", kb, [P, SEQ], F32R) for k, kb in enumerate(OUT_KB[n])]
                                    for n in ("y_hi", "y_lo", "wo_hi", "wo_lo"))
        x_r = at("x_r", 132.5, [P, 2, D])
        o_n = at("o_n", 140.5, [P, 2, D])
        g_fin = at("g_fin", 201, [P, D])

        oss = stat[:, 36:40]
        ssq, var, rms, rstd = (stat[:, 8 * i:8 * i + 8] for i in range(4))
        lss, lvar, lrms, lrstd = (stat[:, 32 + 2 * i:34 + 2 * i] for i in range(4))

        def w_col(kind, u):
            c = 48 + 24 * (u % 2) + 4 * kind
            return stat[:, c:c + 4]

        nm_b, sum_b, r_b = stat[:, 40:44], stat[:, 44:48], stat[:, 32:36]

        ps = ctx.enter_context(nc.psum_tensor("ps", [P, 8, HALF], F32))

        s_id = sem("ident_ready")
        s_gmix, s_glat, s_rnat, s_rq, s_sink, s_dist, s_gfin = (
            sem(n) for n in ("g_mix_in", "g_lat_in", "rope_nat_in", "rope_q_in", "sink_in", "dist_in",
                             "g_fin_in"))
        s_x = [sem(f"x_in{i}") for i in range(2)]
        s_wn = [sem(f"wn_in{i}") for i in range(3)]
        s_chain = sem("dve_chain")
        s_ssq, s_var, s_rms, s_xn = sem("ssq_ready"), sem("var_ready"), sem("rms_ready"), sem("xn_ready")
        s_xT, s_hhi, s_hT = sem("xT_done"), sem("hT_hi_ready"), sem("hT_ready")
        s_wnh, s_wnr = sem("wn_hi_ready"), sem("wn_ready")
        s_pA, s_pB = sem("natA_done"), sem("natB_done")
        s_va, s_lss, s_lvar, s_lrms, s_lat = (sem(n) for n in (
            "va_hi_ready", "lat_ssq_ready", "lat_var_ready", "lat_rms_ready", "lat_ready"))
        s_lT, s_lhi, s_latT = sem("lat_transposed"), sem("latT_hi_ready"), sem("latT_ready")
        s_krr = sem("k_rope_ready")
        s_uqi, s_ukvi = sem("uq_in"), sem("ukv_in")
        s_uqh, s_uq, s_ukvh, s_ukv = sem("uq_hi_ready"), sem("uq_ready"), sem("ukv_hi_ready"), sem("ukv_ready")
        s_up, s_upa, s_upd = sem("up_done"), sem("up_copied_act"), sem("up_copied_dve")
        s_st = [sem(f"stage_stored{i}") for i in range(4)]
        s_w = [sem(f"w_in{i}") for i in range(2)]
        s_wh, s_wr = sem("w_hi_ready"), sem("w_ready")
        s_g, s_ga, s_ge = sem("gated_done"), sem("gated_act"), sem("gated_evacuated")
        s_ws, s_wm, s_wnm, s_we, s_wrd, s_wp = (sem(n) for n in (
            "w_scores", "w_max", "w_negmax", "w_exp", "w_recip", "w_probs_pool"))
        s_wpd = sem("w_probs_dve")
        s_wT, s_wTh, s_wTl, s_wpv, s_wol, s_wo, s_wy = (sem(n) for n in (
            "w_transposed", "w_pT_hi", "w_pT_lo", "w_pv", "w_o_lo", "w_o", "w_y"))
        s_h0, s_h0l = sem("head0_hi"), sem("head0_split")
        s_vr, s_krl, s_qki = sem("v_raw_in"), sem("k_rope_in"), sem("qk_raw_in")
        s_sph, s_sph2, s_sp, s_sp2 = sem("qk_hi_split"), sem("v_hi_split"), sem("qk_split"), sem("v_split")
        s_bs, s_bm, s_be, s_br, s_bp = (sem(n) for n in (
            "b_scores", "b_negmax", "b_exp", "b_recip", "b_probs"))
        s_bT, s_bTh, s_bTl, s_bpv, s_bol, s_bo, s_by = (sem(n) for n in (
            "b_transposed", "b_pT_hi", "b_pT_lo", "b_pv", "b_o_lo", "b_o", "b_y"))
        s_woi = [sem(f"wo_in{i}") for i in range(4)]
        s_yh, s_yl, s_woh, s_wol2 = sem("y_hi_ready"), sem("y_ready"), sem("wo_hi_ready"), sem("wo_ready")
        s_o01 = sem("first_tiles_split")
        s_xr = [sem(f"x_again{i}") for i in range(2)]
        s_op, s_oadd, s_oss, s_ogain, s_ovar, s_orms, s_orstd, s_on0, s_on1 = (sem(n) for n in (
            "out_projected", "out_added", "out_ssq", "out_gained", "out_var", "out_rms", "out_rstd", "out_half0",
            "out_half1"))
        s_out = [sem(f"out_stored{i}") for i in range(2)]

        UP = []
        for half in range(2):
            UP += [("q", j, half) for j in range(4)] + [("r", 0, half), ("r", 1, half), ("kr", 0, half)]
        UP += [("k", j, half) for j in range(4) for half in range(2)]
        UP += [("v", t, 0) for t in range(NT)]
        UP_BANK = (6, 7, 2, 3, 4, 5, 0, 1)
        BY_DVE = ("r", "v")
        UP_LAST = [max(j for j in range(len(UP)) if UP_BANK[j % 8] == b) for b in (6, 7)]
        N_Q = 1 + max(j for j, job in enumerate(UP) if job[0] in ("q", "r"))

        def wait_up_copied(eng, j):
            dve = UP[j][0] in BY_DVE
            n = sum(1 for k in UP[:j + 1] if (k[0] in BY_DVE) == dve)
            if UP[j][0] == "r" and UP[j][1] == 0:
                n += 1
            eng.wait_ge(s_upd if dve else s_upa, n)

        def wait_all_stored(eng):
            for i in range(4):
                eng.wait_ge(s_st[i], 16 * len(range(i, len(UP), 4)))

        M_COLS = [KA] + [QA + P * i for i in range(4)] + [GA + P * i for i in range(4)] \
            + [GB + P * i for i in range(4)]
        NM = len(M_COLS)
        N_WIN_JOB = 2 * (NM - 5)

        def beside(s):
            if s == 0:
                return N_WIN_JOB, range(KT)
            return N_WIN_JOB + (s + 1) // 2, range(4 * ((s + 1) % 2), 4 * ((s + 1) % 2) + 4)

        def g_bank(g):
            return 6 + g % 2 if g < N_WIN_JOB else 6

        def w_keys(u):
            n = u // GROUPS
            return range(max(n - 1, 0), min(n + 2, NT))

        W_UNITS = NT * GROUPS
        W_FIRST = [sum(len(w_keys(v)) for v in range(u)) for u in range(W_UNITS + 1)]

        B_UNITS = HEADS * NT
        B_GROUPS = B_UNITS // 4

        def nat_banks(t):
            return 2 + 2 * (t % 3), 3 + 2 * (t % 3)

        block = ctx.enter_context(nc.Block())

        @block.sync
        def _(sp):
            def load_x(t):
                if t >= 2:
                    sp.wait_ge(s_xn, t - 1)
                sp.dma_start(x_in[:, t % 2, :], x[t * P:(t + 1) * P, :]).then_inc(s_x[t % 2], 16)

            def load_wn(k):
                if k >= 3:
                    sp.wait_ge(s_wnr, k - 2)
                rows = w_in[k * P:(k + 1) * P, :]
                sp.dma_start(wn_raw[:, k % 3, 0:P], rows[:, VA:VA + P]).then_inc(s_wn[k % 3], 16)
                sp.dma_start(wn_raw[:, k % 3, P:NA], rows[:, CKV:CKV + KVL + ROPE]).then_inc(s_wn[k % 3], 16)
                sp.dma_start(wn_raw[:, k % 3, NA:NW], rows[:, CQ:CQ + QL]).then_inc(s_wn[k % 3], 16)

            load_x(0)
            sp.dma_start(g_mix[:, :], norm_mix.partition_broadcast(P)).then_inc(s_gmix, 16)
            load_x(1)
            load_wn(0)
            load_wn(1)
            load_x(2)
            load_wn(2)
            for t in range(3, NT):
                load_wn(t)
                load_x(t)
            sp.dma_start(g_lat[:, 0:QL], q_a_norm.partition_broadcast(P)).then_inc(s_glat, 16)
            sp.dma_start(g_lat[:, QL:QL + KVL], kv_a_norm.partition_broadcast(P)).then_inc(s_glat, 16)
            sp.dma_start(r_nat[:, :, :, :], rope_nat).then_inc(s_rnat, 16)
            sp.dma_start(sinkb[:, :], attn_sink.partition_broadcast(P)).then_inc(s_sink, 16)
            sp.wait_ge(s_wnr, KT)
            sp.dma_start(uq_raw[:, :, :, :],
                         w_uq.rearrange("(k p) (h c) -> p k h c", p=P, c=QK)).then_inc(s_uqi, 16)
            sp.wait_ge(s_pB, NT)
            sp.dma_start(ukv_raw[:, :, :, :],
                         w_ukv.rearrange("(k p) (h c) -> p k h c", p=P, c=P)).then_inc(s_ukvi, 16)
            sp.dma_start(r_q[:, :, :], rope_q).then_inc(s_rq, 16)

            def load_w(m):
                if m >= 2:
                    sp.wait_ge(s_wr, m - 1)
                elif m == 0:
                    sp.wait_ge(s_uq, 1)
                sp.dma_start(w_raw[:, m % 2, :, :],
                             w_in[:, M_COLS[m]:M_COLS[m] + P].rearrange("(k p) c -> p k c", p=P)) \
                    .then_inc(s_w[m % 2], 16)

            load_w(0)
            load_w(1)
            for j, (kind, t, h) in enumerate(UP):
                wait_up_copied(sp, j)
                src, cols = stage[:, j % 4, :], slice(h * HALF, (h + 1) * HALF)
                if kind == "r":
                    dst = qr_scr[t, :, cols]
                elif kind == "q":
                    dst = q_scr[t * P:(t + 1) * P, cols]
                elif kind == "kr":
                    dst, src = kr_scr[:, cols], stage[0:ROPE, j % 4, :]
                elif kind == "k":
                    dst = k_scr[t * P:(t + 1) * P, cols]
                else:
                    dst = v_scr[t * P:(t + 1) * P, :]
                sp.dma_start(dst, src).then_inc(s_st[j % 4], 16)
            sp.wait_ge(s_hT, 2 * NT)
            sp.dma_start(distb[:, :], dist).then_inc(s_dist, 16)
            for m in range(2, NM):
                load_w(m)

            wait_all_stored(sp)
            sp.wait_ge(s_wr, NM)
            sp.dma_start(k_raw[HD:QK, :], kr_scr).then_inc(s_krl, 16)

            def load_qk(h):
                if h >= 2:
                    sp.wait_ge(s_sp, 2 * (h - 1))
                elif h == 1:
                    sp.wait_ge(s_h0l, 2)
                sp.dma_start(q_raw[0:HD, :], q_scr[h * HD:(h + 1) * HD, :]).then_inc(s_qki, 16)
                for i in range(2):
                    sp.dma_start(q_raw[HD + i * HR:HD + (i + 1) * HR, :],
                                 qr_scr[i, h * HR:(h + 1) * HR, :]).then_inc(s_qki, 16)
                sp.dma_start(k_raw[0:HD, :], k_scr[h * HD:(h + 1) * HD, :]).then_inc(s_qki, 16)

            load_qk(0)
            sp.wait_ge(s_ws, REP * W_UNITS)
            sp.dma_start(v_raw[:, :, :], v_scr.rearrange("(t p) c -> p t c", p=P)).then_inc(s_vr, 16)
            for h in range(1, HEADS):
                load_qk(h)

            def load_wo(k):
                if k in (4, 5):
                    sp.wait_ge(s_o01, k - 3)
                elif k >= 6:
                    sp.wait_ge(s_wol2, k - 5)
                sp.dma_start(wo_raw[:, k % 4, :], w_out[k * P:(k + 1) * P, :]).then_inc(s_woi[k % 4], 16)

            sp.wait_ge(s_wT, W_FIRST[W_UNITS])
            sp.wait_ge(s_wo, W_UNITS)
            for k in range(4):
                load_wo(k)
            sp.dma_start(g_fin[:, :], final_norm.partition_broadcast(P)).then_inc(s_gfin, 16)

            def load_again(t):
                if t == 0:
                    sp.wait_ge(s_bT, 2 * B_UNITS)
                if t >= 2:
                    sp.wait_ge(s_oss, 2 * (t - 1))
                sp.dma_start(x_r[:, t % 2, :], x[t * P:(t + 1) * P, :]).then_inc(s_xr[t % 2], 16)

            for k in (4, 5, 6):
                load_wo(k)
            load_again(0)
            load_wo(7)
            load_again(1)
            for t in range(NT):
                for c in range(2):
                    sp.wait_ge((s_on0, s_on1)[c], t + 1)
                    cols = slice(c * HALF, (c + 1) * HALF)
                    sp.dma_start(out[t * P:(t + 1) * P, cols], o_n[:, t % 2, cols]).then_inc(s_out[t % 2], 16)
                if t + 2 < NT:
                    load_again(t + 2)
            for i in range(2):
                sp.wait_ge(s_out[i], 32 * NT // 2)

        @block.gpsimd
        def _(pool):
            def split(raw, hi, lo, done_hi, n_hi, done):
                nc.gpsimd.tensor_scalar(hi, raw, 1.0, 1.0, ALU.mult, ALU.mult).then_inc(done_hi, 1)
                pool.wait_ge(done_hi, n_hi)
                last = nc.gpsimd.tensor_tensor(lo, raw, f(hi), ALU.subtract)
                if done is not None:
                    last.then_inc(done, 1)
                return last

            nc.gpsimd.memset(ident[:, :], 0.0).then_inc(s_id, 1)
            pool.wait_ge(s_id, 1)
            nc.gpsimd.affine_select(out=ident[:, :], in_=ident[:, :], compare_op=ALU.not_equal, fill=1.0,
                                    base=0, pattern=[[-1, P]], channel_multiplier=1).then_inc(s_id, 1)
            for k in range(KT):
                pool.wait_ge(s_wn[k % 3], 48 * (k // 3 + 1))
                split(wn_raw[:, k % 3, :], wn_hi[:, k, :], wn_lo[:, k, :], s_wnh, k + 1, s_wnr)
            pool.wait_ge(s_uqi, 16)
            pool.wait_ge(s_xT, 2 * NT)
            for part in range(2):
                for k in range(QLT):
                    for dst, c, w in ((slice(0, 4), 0, HD), (4, HD, HR), (5, HD + HR, HR)):
                        hi, lo = uq_hi[:, k, dst, :], uq_lo[:, k, dst, :]
                        if w == HD:
                            hi, lo = (a.rearrange("p a (b c) -> p (a b) c", c=w) for a in (hi, lo))
                        else:
                            hi, lo = (a.rearrange("p (b c) -> p b c", c=w) for a in (hi, lo))
                        raw = uq_raw[:, k, :, c:c + w]
                        if part == 0:
                            last = nc.gpsimd.tensor_scalar(hi, raw, 1.0, 1.0, ALU.mult, ALU.mult)
                        else:
                            last = nc.gpsimd.tensor_tensor(lo, raw, f(hi), ALU.subtract)
                last.then_inc(s_uqh if part == 0 else s_uq, 1)
                if part == 0:
                    pool.wait_ge(s_uqh, 1)
            pool.wait_ge(s_ukvi, 16)
            for part in range(2):
                for k in range(KVLT):
                    for hi, lo, c in ((uk_hi, uk_lo, 0), (uv_hi, uv_lo, HD)):
                        raw = ukv_raw[:, k, :, c:c + HD]
                        if part == 0:
                            last = nc.gpsimd.tensor_scalar(hi[:, k, :, :], raw, 1.0, 1.0, ALU.mult, ALU.mult)
                        else:
                            last = nc.gpsimd.tensor_tensor(lo[:, k, :, :], raw, f(hi[:, k, :, :]), ALU.subtract)
                last.then_inc(s_ukvh if part == 0 else s_ukv, 1)
                if part == 0:
                    pool.wait_ge(s_ukvh, 1)

            def split_w(m):
                pool.wait_ge(s_w[m % 2], 16 * (m // 2 + 1))
                if m < 2:
                    pool.wait_ge(s_up, N_Q)
                else:
                    pool.wait_ge(s_g, 2 * (m - 1))
                split(w_raw[:, m % 2, :, :], w_hi[:, m % 2, :, :], w_lo[:, m % 2, :, :], s_wh, m + 1, s_wr)

            def probs_w(u):
                pool.wait_ge(s_wrd, u + 1)
                w = len(w_keys(u)) * P
                for r in range(POOL_R):
                    nc.gpsimd.tensor_scalar(p_w[:, u % 2, r, 0:w], p_w[:, u % 2, r, 0:w], w_col(5, u)[:, r:r + 1],
                                            0.5, ALU.mult, ALU.mult).then_inc(s_wp, 1)

            def gate_w(u):
                n, g = u // GROUPS, u % GROUPS
                if g == 0:
                    pool.wait_ge(s_ge, N_WIN_JOB)
                else:
                    pool.wait_ge(s_ge, N_WIN_JOB + 1 + (n >= NT // 2))
                pool.wait_ge(s_wo, u + 1)
                y = Y[:, 2 * g:2 * g + 2, n * P:(n + 1) * P]
                nc.gpsimd.tensor_tensor(y, y, o_w[:, u % 2, :, :], ALU.mult).then_inc(s_wy, 1)

            for m in range(NM - 3):
                split_w(m)
            for s in range(W_UNITS + 2):
                if s < W_UNITS:
                    probs_w(s)
                if s == W_UNITS:
                    pool.wait_ge(s_h0, 1)
                    nc.gpsimd.tensor_tensor(k_lo[:, 0, :], k_raw[:, :], f(k_hi[:, 0, :]),
                                            ALU.subtract).then_inc(s_h0l, 1)
                if s >= 2:
                    gate_w(s - 2)
                if s in (3, 7, 11):
                    split_w(NM - 3 + (s - 3) // 4)

            def split_piece(h, i):
                hp = h % 2
                if i in (0, 3):
                    raw, hi = (q_raw, q_hi) if i == 0 else (k_raw, k_hi)
                    if i == 0:
                        pool.wait_ge(s_qki, 64 * (h + 1))
                        if h >= 2:
                            pool.wait_ge(s_bs, NT * (h - 1))
                    nc.gpsimd.tensor_scalar(hi[:, hp, :], raw[:, :], 1.0, 1.0, ALU.mult,
                                            ALU.mult).then_inc(s_sph, 1)
                elif i < 6:
                    raw, hi, lo = (q_raw, q_hi, q_lo) if i < 3 else (k_raw, k_hi, k_lo)
                    if i in (1, 4):
                        pool.wait_ge(s_sph, 2 * (h - 1) + 1 + (i == 4))
                    c = slice((i - 1) % 3 * HALF, ((i - 1) % 3 + 1) * HALF)
                    last = nc.gpsimd.tensor_tensor(lo[:, hp, c], raw[:, c], f(hi[:, hp, c]), ALU.subtract)
                    if i in (2, 5):
                        last.then_inc(s_sp, 1)
                elif i == 7:
                    if h == 1:
                        pool.wait_ge(s_sp2, 1)
                    if h >= 2:
                        pool.wait_ge(s_bpv, 2 * (h - 1))
                    raw = v_raw[:, :, h * HD:(h + 1) * HD]
                    split(raw, vB[:, hp, :, 0:HD], vB[:, hp, :, HD:P], s_sph2, h + 1, s_sp2)

            def probs_b(U):
                pool.wait_ge(s_br, U + 1)
                nc.gpsimd.tensor_scalar(p_b[:, (U + 1) % 4, :], p_b[:, (U + 1) % 4, :], r_b[:, U % 4:U % 4 + 1], 0.5,
                                        ALU.mult, ALU.mult).then_inc(s_bp, 1)

            def gate_b(j, c):
                pool.wait_ge(s_bo, 4 * j + c + 3)
                if j == 0 and c == 0:
                    pool.wait_ge(s_ge, 2 * NM)
                y = Y[:, 4 + j, c * HALF:(c + 1) * HALF]
                nc.gpsimd.tensor_tensor(y, y, o_b[:, c, :], ALU.mult).then_inc(s_by, 1)

            def wo_hi_k(k):
                pool.wait_ge(s_woi[k % 4], 16 * (k // 4 + 1))
                nc.gpsimd.tensor_scalar(wo_hi[k][:, :], wo_raw[:, k % 4, :], 1.0, 1.0, ALU.mult, ALU.mult) \
                    .then_inc(s_woh, 1)

            def first_piece(k, i):
                cols = slice((i + 1) % 2 * HALF, ((i + 1) % 2 + 1) * HALF)
                if i == 0:
                    pool.wait_ge(s_sp, 2 * (HEADS - 1))
                    pool.wait_ge(s_sp2, HEADS)
                    wo_hi_k(k)
                elif i < 3:
                    pool.wait_ge(s_woh, k + 1)
                    nc.gpsimd.tensor_tensor(wo_lo[k][:, cols], wo_raw[:, k % 4, cols], f(wo_hi[k][:, cols]),
                                            ALU.subtract)
                else:
                    pool.wait_ge(s_yh, k + 1)
                    last = nc.gpsimd.tensor_tensor(y_lo[k][:, cols], Y[:, k, cols], f(y_hi[k][:, cols]),
                                                   ALU.subtract)
                    if i == 4:
                        last.then_inc(s_o01, 1)

            for U in range(B_UNITS + 8):
                if U < B_UNITS:
                    probs_b(U)
                if U // NT + 1 < HEADS:
                    split_piece(U // NT + 1, U % NT)
                G = (U - 10) // 4
                if U == B_UNITS + 2:
                    wo_hi_k(2)
                    pool.wait_ge(s_bpv, B_GROUPS - 1)
                    wo_hi_k(3)
                    pool.wait_ge(s_bs, B_UNITS)
                    wo_hi_k(4)
                if U >= 10 and (U - 10) % 4 == 0 and G % 4 >= 2:
                    gate_b(G // 4, G % 2)
                if 0 <= U - (B_UNITS - NT) < 10:
                    first_piece((U - (B_UNITS - NT)) // 5, (U - (B_UNITS - NT)) % 5)
            wo_hi_k(5)
            pool.wait_ge(s_bpv, B_GROUPS)
            wo_hi_k(6)
            wo_hi_k(7)

        @block.scalar
        def _(act):
            def h_hi(t):
                for a in range(2):
                    act.wait_ge(s_xT, 2 * t + a + 1)
                    nc.scalar.activation(hT_hi[:, 4 * a:4 * a + 4, t * P:(t + 1) * P],
                                         ps[:, a, :].rearrange("p (k c) -> p k c", c=P),
                                         ACT.Copy).then_inc(s_hhi, 1)

            act.wait_ge(s_id, 2)
            nc.scalar.activation(oss[:, 0:1], ident[:, 0:1], ACT.Sqrt)
            for t in range(NT):
                if t == 3:
                    h_hi(t - 1)
                act.wait_ge(s_x[t % 2], 16 * (t // 2 + 1))
                if t >= 2:
                    act.wait_ge(s_xT, 2 * (t - 1))
                nc.scalar.activation(x_n[:, t % 2, :], x_in[:, t % 2, :], ACT.Square,
                                     accum_out=ssq[:, t:t + 1]).then_inc(s_ssq, 1)
                act.wait_ge(s_var, t + 1)
                nc.scalar.activation(rms[:, t:t + 1], var[:, t:t + 1], ACT.Sqrt).then_inc(s_rms, 1)
                if t >= 1 and t != 3:
                    h_hi(t - 1)
            h_hi(NT - 1)

            def lat_hi(t):
                act.wait_ge(s_lT, t + 1)
                nc.scalar.activation(latT_hi[:, 0:4, t * P:(t + 1) * P],
                                     ps[:, 0, :].rearrange("p (k c) -> p k c", c=P), ACT.Copy)
                nc.scalar.activation(latT_hi[:, 4, t * P:(t + 1) * P], ps[:, 1, 0:P],
                                     ACT.Copy).then_inc(s_lhi, 1)

            for t in range(NT):
                a, b = nat_banks(t)
                act.wait_ge(s_pA, t + 1)
                nc.scalar.activation(vA[:, t, :, 0:HD], ps[:, a, 0:P].rearrange("p (g c) -> p g c", c=HD),
                                     ACT.Copy)
                if t >= 2:
                    act.wait_ge(s_lT, t - 1)
                nc.scalar.activation(lat[:, t % 2, QL:QL + KVL], ps[:, a, P:P + KVL], ACT.Square,
                                     accum_out=lss[:, 1:2])
                nc.scalar.activation(kr_n[:, t, :], ps[:, a, P + KVL:NA], ACT.Copy).then_inc(s_va, 1)
                act.wait_ge(s_pB, t + 1)
                nc.scalar.activation(lat[:, t % 2, 0:QL], ps[:, b, 0:QL], ACT.Square,
                                     accum_out=lss[:, 0:1]).then_inc(s_lss, 1)
                if t >= 2:
                    lat_hi(t - 2)
                act.wait_ge(s_lvar, t + 1)
                nc.scalar.activation(lrms, lvar, ACT.Sqrt).then_inc(s_lrms, 1)
            lat_hi(NT - 2)
            lat_hi(NT - 1)

            for j, (kind, t, h) in enumerate(UP):
                if kind in BY_DVE:
                    continue
                act.wait_ge(s_up, j + 1)
                if j >= 4:
                    act.wait_ge(s_st[j % 4], 16 * (j // 4))
                n = ROPE if kind == "kr" else P
                if kind == "q":
                    nc.scalar.activation(stage[:, j % 4, :], ps[:, UP_BANK[j % 8], :], ACT.Copy,
                                         scale=B_SCALE).then_inc(s_upa, 1)
                else:
                    nc.scalar.activation(stage[0:n, j % 4, :], ps[0:n, UP_BANK[j % 8], :],
                                         ACT.Copy).then_inc(s_upa, 1)

            def evac_g(g):
                m, cols, bank = g // 2, slice(g % 2 * HALF, (g % 2 + 1) * HALF), g_bank(g)
                act.wait_ge(s_g, g + 1)
                if m == 0:
                    wait_all_stored(act)
                    for q in range(GROUPS):
                        for half in (0, HD):
                            last = nc.scalar.activation(k_hi2[half:half + HD, q, cols],
                                                        ps[HD * q:HD * (q + 1), bank, :], ACT.Copy)
                elif m < 5:
                    for q in range(2):
                        h = 2 * (m - 1) + q
                        last = nc.scalar.activation(q_st[0:HD, h, cols], ps[HD * q:HD * (q + 1), bank, :],
                                                    ACT.Copy, scale=-A_SCALE / SLOPE[h])
                else:
                    last = nc.scalar.activation(Y[:, m - 5, cols], ps[:, bank, :], ACT.Tanh, scale=0.5)
                last.then_inc(s_ga, 1)

            def exp_w(u, r):
                w = len(w_keys(u)) * P
                act.wait_ge(s_wm, REP * u + r + 1)
                p = p_w[:, u % 2, r, 0:w]
                nc.scalar.activation(p, p, ACT.Exp, bias=w_col(0, u)[:, r:r + 1], scale=-1.0,
                                     accum_out=w_col(3, u)[:, r:r + 1])

            def exp_sink_w(u):
                act.wait_ge(s_wnm, u + 1)
                nc.scalar.activation(w_col(4, u), w_col(2, u), ACT.Exp).then_inc(s_we, 1)

            def pT_w_hi(c):
                act.wait_ge(s_wT, c + 1)
                if c >= 2:
                    act.wait_ge(s_wpv, c - 1)
                nc.scalar.activation(pT_wh[:, c % 2, :], ps[:, 4 + c % 2, :], ACT.Copy).then_inc(s_wTh, 1)

            def o_w_lo(u):
                act.wait_ge(s_wpv, W_FIRST[u + 1])
                if u >= 1:
                    act.wait_ge(s_wo, u)
                nc.scalar.activation(ol_w[:, :], ps[HD:P, 7, :], ACT.Copy).then_inc(s_wol, 1)

            for g in range(N_WIN_JOB):
                evac_g(g)
            def head0_hi():
                act.wait_ge(s_qki, 64)
                act.wait_ge(s_krl, 16)
                act.wait_ge(s_ws, REP * W_UNITS)
                nc.scalar.activation(k_hi[:, 0, :], k_raw[:, :], ACT.Copy).then_inc(s_h0, 1)
                nc.scalar.activation(q_hi[:, 0, :], q_raw[:, :], ACT.Copy).then_inc(s_h0, 1)

            for s in range(W_UNITS + 1):
                keys = range(W_FIRST[s - 1], W_FIRST[s]) if s >= 1 else []
                live = s < W_UNITS
                if s >= 2:
                    o_w_lo(s - 2)
                if live:
                    exp_w(s, 0)
                else:
                    head0_hi()
                for i, c in enumerate(keys[:2]):
                    pT_w_hi(c)
                    if live:
                        exp_w(s, 1 + i)
                if live:
                    for r in range(1 + len(keys[:2]), REP):
                        exp_w(s, r)
                    exp_sink_w(s)
                for c in keys[2:]:
                    pT_w_hi(c)
                if s % 2 == 0:
                    evac_g(N_WIN_JOB + s // 2)
            o_w_lo(W_UNITS - 1)

            def exp_b(U):
                act.wait_ge(s_bm, U + 1)
                if U >= 4:
                    act.wait_ge(s_bT, 2 * (U - 3))
                b = 2 * (U % 2)
                nc.scalar.activation(p_b[:, (U + 1) % 4, :], ps[:, b:b + 2, :].rearrange("p b c -> p (b c)"), ACT.Exp,
                                     bias=nm_b[:, U % 4:U % 4 + 1],
                                     accum_out=sum_b[:, U % 4:U % 4 + 1]).then_inc(s_be, 1)

            def pT_b_hi(U, a):
                act.wait_ge(s_bT, 2 * U + a + 1)
                G = U // 4
                if U % 4 == 0 and a == 0 and G >= 2:
                    act.wait_ge(s_bpv, G - 1)
                nc.scalar.activation(pT_hi[:, G % 2, 4 * a:4 * a + 4, U % 4 * P:(U % 4 + 1) * P],
                                     ps[:, 4 + a, :].rearrange("p (k c) -> p k c", c=P),
                                     ACT.Copy).then_inc(s_bTh, 1)

            def o_b_lo(G):
                act.wait_ge(s_bpv, G + 1)
                if G >= 1:
                    act.wait_ge(s_bo, G)
                nc.scalar.activation(ol_b[:, :], ps[HD:P, 6 + G % 2, :], ACT.Copy).then_inc(s_bol, 1)

            def y_hi_part(k, c):
                if k == 0 and c == 0:
                    act.wait_ge(s_wy, W_UNITS)
                    act.wait_ge(s_bs, B_UNITS - NT)
                elif k >= 4 and c == 0:
                    act.wait_ge(s_by, 2 * (k - 3))
                cols = slice(c * HALF, (c + 1) * HALF)
                last = nc.scalar.activation(y_hi[k][:, cols], Y[:, k, cols], ACT.Copy)
                if c == 1:
                    last.then_inc(s_yh, 1)

            for U in range(B_UNITS + 7):
                if U == 2:
                    act.wait_ge(s_vr, 16)
                    act.wait_ge(s_g, 2 * NM)
                    nc.scalar.activation(vB[:, 0, :, 0:HD], v_raw[:, :, 0:HD], ACT.Copy).then_inc(s_sph2, 1)
                    evac_g(2 * NM - 1)
                if 2 <= U < B_UNITS + 2:
                    pT_b_hi(U - 2, 0)
                    pT_b_hi(U - 2, 1)
                if U < B_UNITS:
                    exp_b(U)
                if U in (B_UNITS - 8, B_UNITS - 7, B_UNITS - 5, B_UNITS - 4):
                    y_hi_part((U - (B_UNITS - 8)) // 3, (U - (B_UNITS - 8)) % 3)
                if U == B_UNITS:
                    for c in range(2):
                        y_hi_part(2, c)
                if U >= 9 and (U - 9) % 4 == 0:
                    o_b_lo((U - 9) // 4)
                if U == B_UNITS + 2:
                    act.wait_ge(s_bpv, B_GROUPS - 1)
                    act.wait_ge(s_bs, B_UNITS)
                    for k in (3, 4, 5):
                        for c in range(2):
                            y_hi_part(k, c)

            for k in (6, 7):
                for c in range(2):
                    y_hi_part(k, c)
            for t in range(NT):
                for c in range(2):
                    act.wait_ge(s_oadd, 2 * t + c + 1)
                    cols = slice(c * HALF, (c + 1) * HALF)
                    nc.scalar.activation(x_r[:, t % 2, cols], o_n[:, t % 2, cols], ACT.Square, scale=D ** -0.5,
                                         accum_out=oss[:, 2 * (t % 2) + c:2 * (t % 2) + c + 1]).then_inc(s_oss, 1)
                act.wait_ge(s_ovar, t + 1)
                nc.scalar.activation(rms[:, t:t + 1], var[:, t:t + 1], ACT.Sqrt).then_inc(s_orms, 1)
                act.wait_ge(s_ogain, t + 1)
                act.wait_ge(s_orstd, t + 1)
                nc.scalar.activation(o_n[:, t % 2, 0:HALF], o_n[:, t % 2, 0:HALF], ACT.Copy,
                                     scale=rstd[:, t:t + 1]).then_inc(s_on0, 1)

        @block.vector
        def _(dve):
            chain = [0]

            def link(ins):
                chain[0] += 1
                ins.then_inc(s_chain, 1)
                dve.wait_ge(s_chain, chain[0])

            def h_lo(t):
                for a in range(2):
                    dve.wait_ge(s_hhi, 2 * t + a + 1)
                    nc.vector.tensor_tensor(hT_lo[:, 4 * a:4 * a + 4, t * P:(t + 1) * P],
                                            ps[:, a, :].rearrange("p (k c) -> p k c", c=P),
                                            f(hT_hi[:, 4 * a:4 * a + 4, t * P:(t + 1) * P]),
                                            ALU.subtract).then_inc(s_hT, 1)

            for t in range(NT):
                if t == 3:
                    h_lo(t - 1)
                dve.wait_ge(s_ssq, t + 1)
                nc.vector.tensor_scalar(var[:, t:t + 1], ssq[:, t:t + 1], 1.0 / D, EPS, ALU.mult,
                                        ALU.add).then_inc(s_var, 1)
                dve.wait_ge(s_rms, t + 1)
                link(nc.vector.reciprocal(rstd[:, t:t + 1], rms[:, t:t + 1]))
                if t == 0:
                    dve.wait_ge(s_gmix, 16)
                nc.vector.scalar_tensor_tensor(out=x_n[:, t % 2, :], in0=x_in[:, t % 2, :],
                                               scalar=rstd[:, t:t + 1], in1=g_mix[:, :], op0=ALU.mult,
                                               op1=ALU.mult).then_inc(s_xn, 1)
                if t >= 1 and t != 3:
                    h_lo(t - 1)
            h_lo(NT - 1)

            def lat_lo(t):
                dve.wait_ge(s_lhi, t + 1)
                cols = slice(t * P, (t + 1) * P)
                nc.vector.tensor_tensor(latT_lo[:, 0:4, cols], ps[:, 0, :].rearrange("p (k c) -> p k c", c=P),
                                        f(latT_hi[:, 0:4, cols]), ALU.subtract)
                nc.vector.tensor_tensor(latT_lo[:, 4, cols], ps[:, 1, 0:P], f(latT_hi[:, 4, cols]),
                                        ALU.subtract).then_inc(s_latT, 1)

            dve.wait_ge(s_glat, 32)
            for t in range(NT):
                a, b = nat_banks(t)
                dve.wait_ge(s_va, t + 1)
                nc.vector.tensor_tensor(vA[:, t, :, HD:P], ps[:, a, 0:P].rearrange("p (g c) -> p g c", c=HD),
                                        f(vA[:, t, :, 0:HD]), ALU.subtract)
                dve.wait_ge(s_lss, t + 1)
                nc.vector.tensor_scalar(lvar[:, 0:1], lss[:, 0:1], 1.0 / QL, EPS, ALU.mult, ALU.add)
                nc.vector.tensor_scalar(lvar[:, 1:2], lss[:, 1:2], 1.0 / KVL, EPS, ALU.mult,
                                        ALU.add).then_inc(s_lvar, 1)
                if t >= 2:
                    lat_lo(t - 2)
                dve.wait_ge(s_lrms, t + 1)
                link(nc.vector.reciprocal(lrstd, lrms))
                nc.vector.scalar_tensor_tensor(out=lat[:, t % 2, 0:QL], in0=ps[:, b, 0:QL],
                                               scalar=lrstd[:, 0:1], in1=g_lat[:, 0:QL], op0=ALU.mult,
                                               op1=ALU.mult)
                nc.vector.scalar_tensor_tensor(out=lat[:, t % 2, QL:QL + KVL], in0=ps[:, a, P:P + KVL],
                                               scalar=lrstd[:, 1:2], in1=g_lat[:, QL:QL + KVL],
                                               op0=ALU.mult, op1=ALU.mult).then_inc(s_lat, 1)
            lat_lo(NT - 2)
            lat_lo(NT - 1)
            dve.wait_ge(s_rnat, 16)
            x1, x2, cos, sin = kr_n[:, :, 0:HR], kr_n[:, :, HR:ROPE], r_nat[:, 0, :, :], r_nat[:, 1, :, :]
            for i, (a, b) in enumerate(((x1, cos), (x2, sin), (x1, sin), (x2, cos))):
                last = nc.vector.tensor_tensor(kr_t[:, i, :, :], a, b, ALU.mult)
            link(last)
            nc.vector.tensor_tensor(kr_r[:, :, 0:HR], kr_t[:, 0, :, :], kr_t[:, 1, :, :], ALU.subtract)
            nc.vector.tensor_tensor(kr_r[:, :, HR:ROPE], kr_t[:, 2, :, :], kr_t[:, 3, :, :],
                                    ALU.add).then_inc(s_krr, 1)

            dve.wait_ge(s_rq, 16)
            for j, (kind, t, h) in enumerate(UP):
                if kind == "r" and t == 1:
                    x1, x2 = ps[:, UP_BANK[(j - 1) % 8], :], ps[:, UP_BANK[j % 8], :]
                    cos, sin = (r_q[:, i, h * HALF:(h + 1) * HALF] for i in range(2))
                    dve.wait_ge(s_up, j + 1)
                    if h == 1:
                        dve.wait_ge(s_upd, 2)
                    for i in (j - 1, j):
                        dve.wait_ge(s_st[i % 4], 16 * (i // 4))
                    for i, (a, b) in enumerate(((x1, cos), (x2, sin), (x1, sin), (x2, cos))):
                        last = nc.vector.tensor_tensor(r_tmp[:, i, :], a, b, ALU.mult)
                    link(last)
                    nc.vector.tensor_tensor(stage[:, (j - 1) % 4, :], r_tmp[:, 0, :], r_tmp[:, 1, :],
                                            ALU.subtract)
                    nc.vector.tensor_tensor(stage[:, j % 4, :], r_tmp[:, 2, :], r_tmp[:, 3, :],
                                            ALU.add).then_inc(s_upd, 2)
                if kind == "v":
                    dve.wait_ge(s_up, j + 1)
                    dve.wait_ge(s_st[j % 4], 16 * (j // 4))
                    nc.vector.tensor_copy(stage[:, j % 4, :], ps[:, UP_BANK[j % 8], :]).then_inc(s_upd, 1)

            def evac_g(g):
                m, cols, bank = g // 2, slice(g % 2 * HALF, (g % 2 + 1) * HALF), g_bank(g)
                dve.wait_ge(s_ga, g + 1)
                if m == 0:
                    for q in range(GROUPS):
                        for half in (0, HD):
                            last = nc.vector.tensor_tensor(k_lo2[half:half + HD, q, cols],
                                                           ps[HD * q:HD * (q + 1), bank, :],
                                                           f(k_hi2[half:half + HD, q, cols]), ALU.subtract)
                elif m < 5:
                    for q in range(2):
                        h = 2 * (m - 1) + q
                        last = nc.vector.scalar_tensor_tensor(
                            out=q_st[HD:P, h, cols], in0=ps[HD * q:HD * (q + 1), bank, :],
                            scalar=-A_SCALE / SLOPE[h], in1=f(q_st[0:HD, h, cols]), op0=ALU.mult,
                            op1=ALU.subtract)
                else:
                    last = nc.vector.scalar_tensor_tensor(out=Y[:, m - 5, cols], in0=Y[:, m - 5, cols],
                                                          scalar=1.0, in1=ps[:, bank, :], op0=ALU.add,
                                                          op1=ALU.mult)
                last.then_inc(s_ge, 1)

            def max_w(u, r):
                n, g, keys = u // GROUPS, u % GROUPS, w_keys(u)
                c0, w = (keys[0] - (n - 1)) * P, len(keys) * P
                h = REP * g + r
                if u >= 2 and r == 0:
                    dve.wait_ge(s_wT, W_FIRST[u - 1])
                dve.wait_ge(s_ws, REP * u + r + 1)
                nc.vector.tensor_tensor_reduce(out=p_w[:, u % 2, r, 0:w], in0=distb[:, c0:c0 + w],
                                               in1=ps[:, r, 0:w], scale=SLOPE[h],
                                               scalar=nsink[:, h:h + 1], op0=ALU.add, op1=ALU.min,
                                               accum_out=w_col(0, u)[:, r:r + 1]).then_inc(s_wm, 1)

            def sink_w(u):
                g = u % GROUPS
                dve.wait_ge(s_wm, REP * (u + 1))
                nc.vector.tensor_tensor(w_col(2, u), w_col(0, u), nsink[:, REP * g:REP * (g + 1)],
                                        ALU.subtract).then_inc(s_wnm, 1)

            def recip_w(u):
                dve.wait_ge(s_we, u + 1)
                link(nc.vector.tensor_tensor(w_col(4, u), w_col(3, u), w_col(4, u), ALU.add))
                nc.vector.reciprocal(w_col(5, u), w_col(4, u)).then_inc(s_wrd, 1)

            def probs_w(u):
                dve.wait_ge(s_wrd, u + 1)
                w = len(w_keys(u)) * P
                for r in range(POOL_R, REP):
                    last = nc.vector.tensor_scalar(p_w[:, u % 2, r, 0:w], p_w[:, u % 2, r, 0:w],
                                                   w_col(5, u)[:, r:r + 1], 0.5, ALU.mult, ALU.mult)
                last.then_inc(s_wpd, 1)

            def pT_w_lo(c):
                dve.wait_ge(s_wTh, c + 1)
                nc.vector.tensor_tensor(pT_wl[:, c % 2, :], ps[:, 4 + c % 2, :], f(pT_wh[:, c % 2, :]),
                                        ALU.subtract).then_inc(s_wTl, 1)

            def o_w_sum(u):
                dve.wait_ge(s_wol, u + 1)
                if u >= 2:
                    dve.wait_ge(s_wy, u - 1)
                for q in range(2):
                    src = ps[0:HD, 7, :].rearrange("p (a b c) -> p a b c", b=2, c=P)[:, :, q, :]
                    low = ol_w[:, :].rearrange("p (a b c) -> p a b c", b=2, c=P)[:, :, q, :]
                    last = nc.vector.tensor_tensor(o_w[HD * q:HD * (q + 1), u % 2, :, :], src, low, ALU.add)
                last.then_inc(s_wo, 1)

            for g in range(N_WIN_JOB):
                evac_g(g)
            dve.wait_ge(s_dist, 16)
            dve.wait_ge(s_sink, 16)
            link(nc.vector.tensor_scalar(nsink[:, :], sinkb[:, :], -1.0, None, ALU.mult))
            def head0_lo():
                dve.wait_ge(s_h0, 2)
                nc.vector.tensor_tensor(q_lo[:, 0, :], q_raw[:, :], f(q_hi[:, 0, :]), ALU.subtract).then_inc(s_h0l, 1)

            for s in range(W_UNITS + 1):
                keys = range(W_FIRST[s - 1], W_FIRST[s]) if s >= 1 else []
                live = s < W_UNITS
                if live:
                    max_w(s, 0)
                if s >= 2:
                    o_w_sum(s - 2)
                if live:
                    max_w(s, 1)
                    max_w(s, 2)
                if s >= 1:
                    pT_w_lo(keys[0])
                if live:
                    max_w(s, 3)
                    sink_w(s)
                if s >= 1:
                    pT_w_lo(keys[1])
                if live:
                    recip_w(s)
                else:
                    head0_lo()
                for c in keys[2:]:
                    pT_w_lo(c)
                if live:
                    probs_w(s)
                if s % 2 == 0:
                    evac_g(N_WIN_JOB + s // 2)
            o_w_sum(W_UNITS - 1)

            def max_b(U):
                dve.wait_ge(s_bs, U + 1)
                b = 2 * (U % 2)
                nc.vector.tensor_reduce(nm_b[:, U % 4:U % 4 + 1], ps[:, b:b + 2, :].rearrange("p b c -> p (b c)"),
                                        AX.X, ALU.max, negate=True).then_inc(s_bm, 1)

            def recip_b(U):
                dve.wait_ge(s_be, U + 1)
                nc.vector.reciprocal(r_b[:, U % 4:U % 4 + 1], sum_b[:, U % 4:U % 4 + 1]).then_inc(s_br, 1)

            def pT_b_lo(U, a):
                dve.wait_ge(s_bTh, 2 * U + a + 1)
                at_ = (slice(None), U // 4 % 2, slice(4 * a, 4 * a + 4), slice(U % 4 * P, (U % 4 + 1) * P))
                nc.vector.tensor_tensor(pT_lo[at_], ps[:, 4 + a, :].rearrange("p (k c) -> p k c", c=P),
                                        f(pT_hi[at_]), ALU.subtract).then_inc(s_bTl, 1)

            def o_b_sum(G):
                q = HD * (G // 2 % 2)
                dve.wait_ge(s_bol, G + 1)
                if G % 4 < 2 and G >= 4:
                    dve.wait_ge(s_by, 2 * (G // 4 - 1) + G % 2 + 1)
                nc.vector.tensor_tensor(o_b[q:q + HD, G % 2, :], ps[0:HD, 6 + G % 2, :], ol_b[:, :],
                                        ALU.add).then_inc(s_bo, 1)

            def out_lo(k):
                dve.wait_ge(s_yh, k + 1)
                nc.vector.tensor_tensor(y_lo[k][:, :], Y[:, k, :], f(y_hi[k][:, :]), ALU.subtract).then_inc(s_yl, 1)
                dve.wait_ge(s_woh, k + 1)
                nc.vector.tensor_tensor(wo_lo[k][:, :], wo_raw[:, k % 4, :], f(wo_hi[k][:, :]),
                                        ALU.subtract).then_inc(s_wol2, 1)

            for U in range(B_UNITS + 7):
                if 1 <= U <= B_UNITS:
                    recip_b(U - 1)
                if U == 2:
                    dve.wait_ge(s_sph2, 1)
                    nc.vector.tensor_tensor(vB[:, 0, :, HD:P], v_raw[:, :, 0:HD], f(vB[:, 0, :, 0:HD]),
                                            ALU.subtract).then_inc(s_sp2, 1)
                    evac_g(2 * NM - 1)
                if U < B_UNITS:
                    max_b(U)
                if 2 <= U < B_UNITS + 2:
                    pT_b_lo(U - 2, 0)
                    pT_b_lo(U - 2, 1)
                if U >= 9 and (U - 9) % 4 == 0:
                    o_b_sum((U - 9) // 4)
                if U == B_UNITS + 2:
                    out_lo(2)
                    out_lo(3)

            for k in range(4, KT):
                out_lo(k)
            dve.wait_ge(s_gfin, 16)
            for t in range(NT):
                for c in range(2):
                    cols = slice(c * HALF, (c + 1) * HALF)
                    dve.wait_ge(s_op, 2 * t + c + 1)
                    if c == 0:
                        dve.wait_ge(s_xr[t % 2], 16 * (t // 2 + 1))
                        if t >= 2:
                            dve.wait_ge(s_out[t % 2], 32 * (t // 2))
                    nc.vector.tensor_tensor(o_n[:, t % 2, cols], ps[:, 2 * (t % 4) + c, :],
                                            x_r[:, t % 2, cols], ALU.add).then_inc(s_oadd, 1)
                    if c == 0:
                        dve.wait_ge(s_oss, 2 * t + 1)
                        nc.vector.tensor_tensor(o_n[:, t % 2, cols], o_n[:, t % 2, cols], g_fin[:, cols],
                                                ALU.mult).then_inc(s_ogain, 1)
                dve.wait_ge(s_oss, 2 * t + 2)
                nc.vector.tensor_scalar(var[:, t:t + 1], oss[:, 2 * (t % 2):2 * (t % 2) + 1],
                                        oss[:, 2 * (t % 2) + 1:2 * (t % 2) + 2], EPS, ALU.add,
                                        ALU.add).then_inc(s_ovar, 1)
                dve.wait_ge(s_orms, t + 1)
                nc.vector.reciprocal(rstd[:, t:t + 1], rms[:, t:t + 1]).then_inc(s_orstd, 1)
                dve.wait_ge(s_orstd, t + 1)
                nc.vector.scalar_tensor_tensor(out=o_n[:, t % 2, HALF:], in0=o_n[:, t % 2, HALF:],
                                               scalar=rstd[:, t:t + 1], in1=g_fin[:, HALF:], op0=ALU.mult,
                                               op1=ALU.mult).then_inc(s_on1, 1)

        @block.tensor
        def _(pe):
            def three(o, a_hi, a_lo, b_hi, b_lo, first, last):
                nc.tensor.matmul(o, a_hi, b_hi, start=first, stop=False)
                nc.tensor.matmul(o, a_hi, b_lo, start=False, stop=False)
                return nc.tensor.matmul(o, a_lo, b_hi, start=False, stop=last)

            def turn_x(t):
                pe.wait_ge(s_xn, t + 1)
                for a in range(2):
                    if t >= 1:
                        pe.wait_ge(s_hT, 2 * t - 1 + a)
                    for k in range(4):
                        c = 4 * a + k
                        last = nc.tensor.transpose(ps[:, a, k * P:(k + 1) * P], x_n[:, t % 2, c * P:(c + 1) * P],
                                                   ident[:, :])
                    last.then_inc(s_xT, 1)

            def natural(t, c, ks):
                w0, w1 = ((0, NA), (NA, NW))[c]
                toks = slice(t * P, (t + 1) * P)
                for k in ks:
                    last = three(ps[:, nat_banks(t)[c], 0:w1 - w0], hT_hi[:, k, toks], hT_lo[:, k, toks],
                                 wn_hi[:, k, w0:w1], wn_lo[:, k, w0:w1], k == 0, k == KT - 1)
                if ks[-1] == KT - 1:
                    last.then_inc((s_pA, s_pB)[c], 1)

            def turn_lat(t):
                pe.wait_ge(s_lat, t + 1)
                if t == 0:
                    pe.wait_ge(s_hT, 2 * NT)
                else:
                    pe.wait_ge(s_latT, t)
                for k in range(LT):
                    last = nc.tensor.transpose(ps[:, k // 4, k % 4 * P:(k % 4 + 1) * P],
                                               lat[:, t % 2, k * P:(k + 1) * P], ident[:, :])
                last.then_inc(s_lT, 1)

            pe.wait_ge(s_id, 2)
            turn_x(0)
            turn_x(1)
            for k in range(KT - 2):
                for t in range(3):
                    if k == 0:
                        pe.wait_ge(s_hT, 2 * (t + 1))
                    pe.wait_ge(s_wnr, k + 1)
                    for c in range(2):
                        natural(t, c, range(k, k + 1))
                    if k == 0 and t == 0:
                        turn_x(2)
                if k >= 1:
                    turn_x(2 + k)
            pe.wait_ge(s_wnr, KT)
            for t in range(3):
                for c in range(2):
                    natural(t, c, range(KT - 2, KT))
            for t in range(3, NT):
                pe.wait_ge(s_hT, 2 * (t + 1))
                pe.wait_ge(s_lat, t - 2)
                natural(t, 0, range(KT))
                if t == 3:
                    turn_lat(0)
                natural(t, 1, range(KT))
                turn_lat(t - 2)

            for j, (kind, t, h) in enumerate(UP):
                o = ps[:, UP_BANK[j % 8], :]
                cols = slice(h * HALF, (h + 1) * HALF)
                if j in (2, 3):
                    turn_lat(j + 4)
                if j == 0:
                    pe.wait_ge(s_latT, 4)
                    pe.wait_ge(s_uq, 1)
                elif j == 2:
                    pe.wait_ge(s_lat, 7)
                if j == 6:
                    pe.wait_ge(s_latT, NT)
                if kind == "kr" and h == 0:
                    pe.wait_ge(s_krr, 1)
                if kind == "k" and t == 0 and h == 0:
                    pe.wait_ge(s_ukv, 1)
                if j >= 8:
                    wait_up_copied(pe, j - 8)
                if kind in ("r", "q"):
                    c = 4 + t if kind == "r" else t
                    for k in range(QLT):
                        last = three(o, uq_hi[:, k, c, :], uq_lo[:, k, c, :], latT_hi[:, k, cols],
                                     latT_lo[:, k, cols], k == 0, k == QLT - 1)
                elif kind == "kr":
                    for i in range(4):
                        last = nc.tensor.transpose(o[0:ROPE, i * P:(i + 1) * P], kr_r[:, 4 * h + i, :], ident[:, :])
                elif kind == "k":
                    for k in range(KVLT):
                        wh, wl = (a[:, k, 2 * t:2 * t + 2, :].rearrange("p a c -> p (a c)") for a in (uk_hi, uk_lo))
                        last = three(o, wh, wl, latT_hi[:, QLT + k, cols], latT_lo[:, QLT + k, cols],
                                     k == 0, k == KVLT - 1)
                else:
                    toks = slice(t * P, (t + 1) * P)
                    for k in range(KVLT):
                        wh, wl = (a[:, k, :, :].rearrange("p a c -> p (a c)") for a in (uv_hi, uv_lo))
                        last = three(o, latT_hi[:, QLT + k, toks], latT_lo[:, QLT + k, toks], wh, wl,
                                     k == 0, k == KVLT - 1)
                last.then_inc(s_up, 1)

            def gated(g, ks):
                m, cols = g // 2, slice(g % 2 * HALF, (g % 2 + 1) * HALF)
                if ks[0] == 0:
                    pe.wait_ge(s_wr, m + 1)
                    if g < 2:
                        wait_up_copied(pe, UP_LAST[g])
                    else:
                        pe.wait_ge(s_ge, g if g > N_WIN_JOB else g - 1)
                for k in ks:
                    last = three(ps[:, g_bank(g), :], w_hi[:, m % 2, k, :], w_lo[:, m % 2, k, :],
                                 hT_hi[:, k, cols], hT_lo[:, k, cols], k == 0, k == KT - 1)
                if ks[-1] == KT - 1:
                    last.then_inc(s_g, 1)

            def scores_w(u):
                n, g, keys = u // GROUPS, u % GROUPS, w_keys(u)
                k0, w = keys[0] * P, len(keys) * P
                if u == 0:
                    wait_up_copied(pe, len(UP) - 1)
                for r in range(REP):
                    if u >= 1:
                        pe.wait_ge(s_wm, REP * (u - 1) + r + 1)
                    q = q_st[:, REP * g + r, n * P:(n + 1) * P]
                    nc.tensor.matmul(ps[:, r, 0:w], q, k_hi2[:, g, k0:k0 + w], start=True, stop=False)
                    nc.tensor.matmul(ps[:, r, 0:w], q, k_lo2[:, g, k0:k0 + w], start=False,
                                     stop=True).then_inc(s_ws, 1)

            def turn_w(u, i):
                c = W_FIRST[u] + i
                if i == 0:
                    pe.wait_ge(s_wp, POOL_R * (u + 1))
                    pe.wait_ge(s_wpd, u + 1)
                if c >= 2:
                    pe.wait_ge(s_wTl, c - 1)
                for r in range(REP):
                    last = nc.tensor.transpose(ps[:, 4 + c % 2, r * P:(r + 1) * P],
                                               p_w[:, u % 2, r, i * P:(i + 1) * P], ident[:, :])
                last.then_inc(s_wT, 1)

            def pv_w(u, i):
                c, keys = W_FIRST[u] + i, w_keys(u)
                if i == 0:
                    pe.wait_ge(s_wo, u) if u else pe.wait_ge(s_ge, N_WIN_JOB)
                pe.wait_ge(s_wTl, c + 1)
                v = vA[:, keys[i], u % GROUPS, :]
                nc.tensor.matmul(ps[:, 7, :], v, pT_wh[:, c % 2, :], start=(i == 0), stop=False)
                nc.tensor.matmul(ps[:, 7, :], v, pT_wl[:, c % 2, :], start=False,
                                 stop=(i == len(keys) - 1)).then_inc(s_wpv, 1)

            def scores_b(U):
                h, t, hp = U // NT, U % NT, U // NT % 2
                if t == 0:
                    if h == 0:
                        pe.wait_ge(s_h0l, 2)
                    else:
                        pe.wait_ge(s_sp, 2 * h)
                if U >= 2:
                    pe.wait_ge(s_be, U - 1)
                q = slice(t * P, (t + 1) * P)
                for c in range(2):
                    k = slice(c * HALF, (c + 1) * HALF)
                    last = three(ps[:, 2 * (U % 2) + c, :], q_hi[:, hp, q], q_lo[:, hp, q], k_hi[:, hp, k],
                                 k_lo[:, hp, k], True, True)
                last.then_inc(s_bs, 1)

            for g in range(N_WIN_JOB):
                gated(g, range(KT))
            for s in range(W_UNITS + 1):
                g, ks = beside(s)
                n = len(w_keys(s - 1)) if s >= 1 else 0
                if s < W_UNITS:
                    scores_w(s)
                for i in range(min(n, 2)):
                    turn_w(s - 1, i)
                gated(g, ks[:len(ks) // 2])
                if n:
                    pv_w(s - 1, 0)
                    if n > 2:
                        turn_w(s - 1, 2)
                ks = ks[len(ks) // 2:]
                before = len(ks) if s % 2 == 0 else len(ks) // 2
                gated(g, ks[:before])
                if n:
                    pv_w(s - 1, 1)
                if before < len(ks):
                    gated(g, ks[before:])
                if n > 2:
                    pv_w(s - 1, 2)
            pe.wait_ge(s_wm, REP * W_UNITS)
            scores_b(0)
            scores_b(1)
            gated(2 * NM - 1, range(KT))

            def turn_b(U):
                pe.wait_ge(s_bp, U + 1)
                for a in range(2):
                    if U >= 1:
                        pe.wait_ge(s_bTl, 2 * (U - 1) + a + 1)
                    else:
                        pe.wait_ge(s_wTl, W_FIRST[W_UNITS])
                    for k in range(4):
                        last = nc.tensor.transpose(ps[:, 4 + a, k * P:(k + 1) * P],
                                                   p_b[:, (U + 1) % 4, (4 * a + k) * P:(4 * a + k + 1) * P], ident[:, :])
                    last.then_inc(s_bT, 1)

            def pv_b(G, part):
                hp = G // 2 % 2
                if part == 0:
                    pe.wait_ge(s_sp2, G // 2 + 1)
                    pe.wait_ge(s_bTl, 8 * (G + 1))
                    if G >= 2:
                        pe.wait_ge(s_bo, G - 1)
                    else:
                        pe.wait_ge(s_wo, W_UNITS)
                        pe.wait_ge(s_ge, 2 * NM)
                for k in (2 * part, 2 * part + 1):
                    o = ps[:, 6 + G % 2, :]
                    nc.tensor.matmul(o, vB[:, hp, k, :], pT_hi[:, G % 2, k, :], start=(k == 0), stop=False)
                    last = nc.tensor.matmul(o, vB[:, hp, k, :], pT_lo[:, G % 2, k, :], start=False,
                                            stop=(k == NT - 1))
                if part == 3:
                    last.then_inc(s_bpv, 1)

            def out_proj(k, tiles, halves):
                if tiles[0] == 0 and k < 2:
                    pe.wait_ge(s_o01, k + 1)
                elif tiles[0] == 0:
                    pe.wait_ge(s_yl, k - 1)
                    pe.wait_ge(s_wol2, k - 1)
                for t in tiles:
                    for c in halves:
                        last = three(ps[:, 2 * (t % 4) + c, :], y_hi[k][:, t * P:(t + 1) * P],
                                     y_lo[k][:, t * P:(t + 1) * P], wo_hi[k][:, c * HALF:(c + 1) * HALF],
                                     wo_lo[k][:, c * HALF:(c + 1) * HALF], k == 0, k == KT - 1)
                        if k == KT - 1:
                            last.then_inc(s_op, 1)

            for U in range(B_UNITS + 6):
                if 2 <= U < B_UNITS:
                    scores_b(U)
                if 2 <= U < B_UNITS + 2:
                    turn_b(U - 2)
                if U >= 6:
                    pv_b((U - 6) // 4, (U - 6) % 4)
                if U == B_UNITS + 1:
                    pe.wait_ge(s_be, B_UNITS)
                    out_proj(0, range(2), range(2))

            out_proj(1, range(2), range(2))
            pe.wait_ge(s_bTl, 2 * B_UNITS)
            out_proj(0, range(2, 3), range(2))
            out_proj(1, range(2, 3), range(2))
            for k in range(2, KT):
                out_proj(k, range(3), range(2))
            for t in range(3, NT):
                if t == 3:
                    pe.wait_ge(s_bo, B_GROUPS)
                for c in range(2):
                    if t >= 4:
                        pe.wait_ge(s_oadd, 2 * (t - 4) + c + 1)
                    for k in range(KT):
                        out_proj(k, range(t, t + 1), range(c, c + 1))


def _constants():
    pos = np.arange(SEQ, dtype=np.float32)
    inv = np.float32(10000.0) ** (-np.arange(0, ROPE, 2, dtype=np.float32) / np.float32(ROPE))
    ang = pos[:, None] * inv[None, :]
    cs = np.stack([np.cos(ang), np.sin(ang)]).astype(np.float32)
    nat = cs.reshape(2, NT, P, HR).transpose(2, 0, 1, 3)
    q = np.tile(cs.transpose(0, 2, 1), (1, HEADS, 1)).transpose(1, 0, 2)
    q = q.astype(np.float64) * B_SCALE
    away = np.abs(np.arange(P)[:, None] - np.arange(3 * P)[None, :] + P)
    dist = np.where(away <= P, away.astype(np.float32), np.float32(MASKED))
    return {"rope_nat": nat.astype(np.float32), "rope_q": q.astype(np.float32),
            "dist": dist.astype(np.float32)}


_INS = ["x", "norm_mix", "w_in", "attn_sink", "q_a_norm", "w_uq", "kv_a_norm", "w_ukv", "w_out", "final_norm"]


def kernel(**inputs):
    import concourse.bacc as _bacc
    from concourse.bass_utils import run_bass_kernel_spmd as _run

    nc = _bacc.Bacc("TRN2", target_bir_lowering=False, num_devices=1)
    arrays, args = {}, {}
    for name in _INS:
        a = np.ascontiguousarray(inputs[name])
        if name != "final_norm":
            a = a[0]
        arrays[name] = np.ascontiguousarray(a)
    for name, a in _constants().items():
        arrays[name] = np.ascontiguousarray(a)
    for name, a in arrays.items():
        args[name] = nc.dram_tensor(name, a.shape, mybir.dt.from_np(a.dtype), kind="ExternalInput").ap()
    out = nc.dram_tensor("out", (SEQ, D), F32, kind="ExternalOutput").ap()
    encoder(nc, out=out, **args)
    r = _run(nc, [arrays], core_ids=[0])
    return r.results[0]["out"].reshape(1, SEQ, D)
```
